# Optimizing a Trainium2 kernel written in Bass

```python
import math
import jax, jax.numpy as jnp
from jax import lax
import numpy as np

D_MODEL = 1024
BATCH = 1
SEQ = 128
DEPTH = 2
DEC_BATCH = 1
DEC_SEQ = 1024
PAST_LEN = 128

GRID_W = 64
Q_BLOCK = 128
ROPE_BASE = 10000.0
EPS = 1e-6
N_MIXERS = 4
GROUP_W = D_MODEL // N_MIXERS
D_MIX = N_MIXERS * GROUP_W
MLA_HEADS = 4
MLA_NOPE = 64
MLA_ROPE = 32
MLA_V = GROUP_W // MLA_HEADS
MLA_Q_RANK = D_MODEL // 4
MLA_KV_RANK = D_MODEL // 8
GQA_HEADS = 4
GQA_KV_HEADS = 2
GQA_HD = GROUP_W // GQA_HEADS
DIFF_HEADS = 4
DIFF_VD = GROUP_W // DIFF_HEADS
DIFF_HD = DIFF_VD // 2
HY_W = GROUP_W
HY_ORDER = 2
HY_CONV = 3
HY_EMB = 33
HY_BANDS = (HY_EMB - 1) // 2
HY_FFN = 64
HY_DECAY_MIN = 3.07
HY_DECAY_MAX = 15.35
SPLIT_SIZES = (MLA_Q_RANK, MLA_KV_RANK, MLA_ROPE, GROUP_W,
               GQA_HEADS * GQA_HD, GQA_KV_HEADS * GQA_HD, GQA_KV_HEADS * GQA_HD, GROUP_W,
               DIFF_HEADS * 2 * DIFF_HD, DIFF_HEADS * 2 * DIFF_HD, DIFF_HEADS * DIFF_VD, GROUP_W,
               3 * HY_W, GROUP_W)
P_IN = sum(SPLIT_SIZES)

kernel_name = 'hybrid_parallel_heads_diffusion_step'

def rmsnorm(x, g):
    xf = x.astype(jnp.float32)
    y = xf * lax.rsqrt(jnp.mean(xf * xf, axis=-1, keepdims=True) + EPS)
    return (y * g.astype(jnp.float32)).astype(x.dtype)

def grid_positions(n_tokens):
    rows = n_tokens // GRID_W
    row = jnp.repeat(jnp.arange(rows, dtype=jnp.float32), GRID_W)
    col = jnp.tile(jnp.arange(GRID_W, dtype=jnp.float32), rows)
    return row, col

def rope_1d(x, pos):
    m = x.shape[-1]
    inv = ROPE_BASE ** (-jnp.arange(0, m, 2, dtype=jnp.float32) / m)
    ang = pos[:, None] * inv[None, :]
    bshape = (1, x.shape[1]) + (1,) * (x.ndim - 3) + (m,)
    cos = jnp.concatenate([jnp.cos(ang), jnp.cos(ang)], axis=-1).reshape(bshape).astype(x.dtype)
    sin = jnp.concatenate([jnp.sin(ang), jnp.sin(ang)], axis=-1).reshape(bshape).astype(x.dtype)
    x1, x2 = jnp.split(x, 2, axis=-1)
    return x * cos + jnp.concatenate([-x2, x1], axis=-1) * sin

def axial_rope(x, row, col):
    half = x.shape[-1] // 2
    return jnp.concatenate([rope_1d(x[..., :half], row), rope_1d(x[..., half:], col)], axis=-1)

def over_query_blocks(fn, q):
    b, lq = q.shape[0], q.shape[1]
    nb = lq // Q_BLOCK
    qb = jnp.swapaxes(q.reshape((b, nb, Q_BLOCK) + q.shape[2:]), 0, 1)
    out = lax.map(fn, qb)
    return jnp.swapaxes(out, 0, 1).reshape((b, lq) + out.shape[3:])

def mha_blocks(q, k, v):
    scale = q.shape[-1] ** -0.5
    def blk(qb):
        s = jnp.einsum('bqhd,bkhd->bhqk', qb, k).astype(jnp.float32) * scale
        p = jax.nn.softmax(s, axis=-1).astype(v.dtype)
        return jnp.einsum('bhqk,bkhd->bqhd', p, v)
    return over_query_blocks(blk, q)

def gqa_blocks(q, k, v):
    scale = q.shape[-1] ** -0.5
    def blk(qb):
        s = jnp.einsum('bqgrd,bkgd->bgrqk', qb, k).astype(jnp.float32) * scale
        p = jax.nn.softmax(s, axis=-1).astype(v.dtype)
        return jnp.einsum('bgrqk,bkgd->bqgrd', p, v)
    return over_query_blocks(blk, q)

def diff_blocks(q, k, v, lam):
    scale = q.shape[-1] ** -0.5
    def blk(qb):
        s = jnp.einsum('bqhsd,bkhsd->bhsqk', qb, k).astype(jnp.float32) * scale
        p = jax.nn.softmax(s, axis=-1)
        a = (p[:, :, 0] - lam * p[:, :, 1]).astype(v.dtype)
        return jnp.einsum('bhqk,bkhd->bqhd', a, v)
    return over_query_blocks(blk, q)

def short_conv(u, w, b):
    n = u.shape[1]
    up = jnp.pad(u, ((0, 0), (1, 1), (0, 0)))
    return up[:, :n] * w[0] + up[:, 1:n + 1] * w[1] + up[:, 2:] * w[2] + b

def hyena_filters(n, lp):
    f32 = jnp.float32
    t = jnp.linspace(0.0, 1.0, n, dtype=f32)[:, None]
    w = 2.0 * math.pi * jnp.arange(n, dtype=f32)[:, None] / n
    f = jnp.linspace(1e-4, HY_BANDS - 1, HY_BANDS, dtype=f32)[None, :]
    feats = jnp.concatenate([t, jnp.cos(f * w), -jnp.sin(f * w)], axis=-1)
    freq = lp['hy_freq'].astype(f32)
    h = jnp.sin(freq[0] * (feats @ lp['hy_fw1'].astype(f32) + lp['hy_fb1'].astype(f32)))
    h = jnp.sin(freq[1] * (h @ lp['hy_fw2'].astype(f32) + lp['hy_fb2'].astype(f32)))
    h = (h @ lp['hy_fw3'].astype(f32)).reshape(n, HY_ORDER, 2, HY_W)
    decay = jnp.exp(-t[:, :, None, None] * jnp.abs(lp['hy_decay'].astype(f32)))
    return h * decay

def bidir_long_conv(u, h_fwd, h_bwd, bias):
    n = u.shape[1]
    filt = jnp.concatenate([h_fwd, jnp.zeros((1, h_fwd.shape[-1]), jnp.float32), h_bwd[1:][::-1]], axis=0)
    uf = u.astype(jnp.float32)
    spec = jnp.fft.rfft(uf, n=2 * n, axis=1) * jnp.fft.rfft(filt, n=2 * n, axis=0)[None]
    y = jnp.fft.irfft(spec, n=2 * n, axis=1)[:, :n]
    return (y + uf * bias.astype(jnp.float32)).astype(u.dtype)

def hyena(u, lp):
    n = u.shape[1]
    x1, x2, v = jnp.split(short_conv(u, lp['hy_conv_w'], lp['hy_conv_b']), 3, axis=-1)
    filt = hyena_filters(n, lp)
    z = v
    for o, g in enumerate((x1, x2)):
        z = g * bidir_long_conv(z, filt[:, o, 0], filt[:, o, 1], lp['hy_bias'][o])
    return z

def mixer(h, lp, layer_idx, ctx):
    b, n, _ = h.shape
    z = h @ lp['w_in']
    (m_cq, m_ckv, m_kr, m_gate, g_q, g_k, g_v, g_gate,
     d_q, d_k, d_v, d_gate, hy_in, hy_gate) = jnp.split(z, np.cumsum(SPLIT_SIZES)[:-1].tolist(), axis=-1)
    q_mla = (rmsnorm(m_cq, lp['mla_q_norm']) @ lp['mla_wq_b']).reshape(b, n, MLA_HEADS, MLA_NOPE + MLA_ROPE)
    q_nope, q_rope = q_mla[..., :MLA_NOPE], q_mla[..., MLA_NOPE:]
    ckv = rmsnorm(m_ckv, lp['mla_kv_norm'])
    kr = m_kr
    gq = rmsnorm(g_q.reshape(b, n, GQA_HEADS, GQA_HD), lp['gqa_q_norm'])
    gk = rmsnorm(g_k.reshape(b, n, GQA_KV_HEADS, GQA_HD), lp['gqa_k_norm'])
    gv = g_v.reshape(b, n, GQA_KV_HEADS, GQA_HD)
    dq = d_q.reshape(b, n, DIFF_HEADS, 2, DIFF_HD)
    dk = d_k.reshape(b, n, DIFF_HEADS, 2, DIFF_HD)
    dv = d_v.reshape(b, n, DIFF_HEADS, DIFF_VD)
    state = (ckv, kr, gk, gv, dk.reshape(b, n, DIFF_HEADS, 2 * DIFF_HD), dv)
    if ctx is None:
        k_ckv, k_kr, k_g, v_g, k_d, v_d = state
    else:
        row, col = grid_positions(n)
        q_rope = axial_rope(q_rope, row, col)
        gq = axial_rope(gq, row, col)
        dq = axial_rope(dq, row, col)
        lat = (ckv, axial_rope(kr, row, col), axial_rope(gk, row, col), gv,
               axial_rope(dk, row, col).reshape(b, n, DIFF_HEADS, 2 * DIFF_HD), dv)
        k_ckv, k_kr, k_g, v_g, k_d, v_d = [jnp.concatenate([cs.astype(ls.dtype), ls], axis=1)
                                           for cs, ls in zip(ctx, lat)]
    kv = (k_ckv @ lp['mla_wkv_b']).reshape(b, -1, MLA_HEADS, MLA_NOPE + MLA_V)
    k_mla = jnp.concatenate([kv[..., :MLA_NOPE],
                             jnp.broadcast_to(k_kr[:, :, None, :], k_kr.shape[:2] + (MLA_HEADS, MLA_ROPE))], axis=-1)
    o_mla = mha_blocks(jnp.concatenate([q_nope, q_rope], axis=-1), k_mla, kv[..., MLA_NOPE:]).reshape(b, n, GROUP_W)
    o_gqa = gqa_blocks(gq.reshape(b, n, GQA_KV_HEADS, GQA_HEADS // GQA_KV_HEADS, GQA_HD), k_g, v_g).reshape(b, n, GROUP_W)
    lam_init = 0.8 - 0.6 * math.exp(-0.3 * layer_idx)
    f32 = jnp.float32
    lam = (jnp.exp(jnp.sum(lp['diff_lq1'].astype(f32) * lp['diff_lk1'].astype(f32)))
           - jnp.exp(jnp.sum(lp['diff_lq2'].astype(f32) * lp['diff_lk2'].astype(f32))) + lam_init)
    o_diff = diff_blocks(dq, k_d.reshape(b, -1, DIFF_HEADS, 2, DIFF_HD), v_d, lam)
    o_diff = (rmsnorm(o_diff, lp['diff_subln']) * (1.0 - lam_init)).reshape(b, n, GROUP_W)
    o_hy = hyena(hy_in, lp)
    o = jnp.concatenate([o_mla * jax.nn.silu(m_gate), o_gqa * jax.nn.silu(g_gate),
                         o_diff * jax.nn.silu(d_gate), o_hy * jax.nn.silu(hy_gate)], axis=-1)
    return o @ lp['w_out'], state

def trunk_layer(x, mod, lp, layer_idx, ctx):
    shift, scale, gate = jnp.split(mod[:, None, :], 3, axis=-1)
    h = rmsnorm(x, lp['norm_pre']) * (1.0 + scale) + shift
    out, state = mixer(h, lp, layer_idx, ctx)
    return x + gate * rmsnorm(out, lp['norm_post']), state

def setup_inputs(seed: int = 0) -> dict:
    key = jax.random.key(seed)
    ks = jax.random.split(key, 40)
    f32 = jnp.float32

    def nrm(i, shape, scale):
        return jax.random.normal(ks[i], shape, f32) * scale

    def gain(i, shape):
        return 1.0 + nrm(i, shape, 0.1)

    decay = jnp.broadcast_to(jnp.linspace(HY_DECAY_MIN, HY_DECAY_MAX, HY_W, dtype=f32), (DEPTH, HY_W)) + nrm(35, (DEPTH, HY_W), 0.1)
    return {
        'x_prompt': nrm(0, (BATCH, SEQ, D_MODEL), 1.0),
        'x_sample': nrm(1, (DEC_BATCH, DEC_SEQ, D_MODEL), 1.0),
        'cache_mla_ckv': nrm(2, (DEC_BATCH, DEPTH, PAST_LEN, MLA_KV_RANK), 1.0),
        'cache_mla_krope': nrm(3, (DEC_BATCH, DEPTH, PAST_LEN, MLA_ROPE), 1.0),
        'cache_gqa_k': nrm(4, (DEC_BATCH, DEPTH, PAST_LEN, GQA_KV_HEADS, GQA_HD), 1.0),
        'cache_gqa_v': nrm(5, (DEC_BATCH, DEPTH, PAST_LEN, GQA_KV_HEADS, GQA_HD), 1.0),
        'cache_diff_k': nrm(6, (DEC_BATCH, DEPTH, PAST_LEN, DIFF_HEADS, 2 * DIFF_HD), 1.0),
        'cache_diff_v': nrm(7, (DEC_BATCH, DEPTH, PAST_LEN, DIFF_HEADS, DIFF_VD), 1.0),
        'c': nrm(8, (DEC_BATCH, D_MODEL), 1.0),
        'c_ctx': nrm(9, (D_MODEL,), 1.0),
        'norm_pre': gain(10, (DEPTH, D_MODEL)),
        'norm_post': gain(11, (DEPTH, D_MODEL)),
        'ada_w': nrm(12, (DEPTH, D_MODEL, 3 * D_MODEL), D_MODEL ** -0.5),
        'ada_b': nrm(13, (DEPTH, 3 * D_MODEL), 0.02),
        'w_in': nrm(14, (DEPTH, D_MODEL, P_IN), D_MODEL ** -0.5),
        'w_out': nrm(15, (DEPTH, D_MIX, D_MODEL), D_MIX ** -0.5),
        'mla_q_norm': gain(16, (DEPTH, MLA_Q_RANK)),
        'mla_wq_b': nrm(17, (DEPTH, MLA_Q_RANK, MLA_HEADS * (MLA_NOPE + MLA_ROPE)), MLA_Q_RANK ** -0.5),
        'mla_kv_norm': gain(18, (DEPTH, MLA_KV_RANK)),
        'mla_wkv_b': nrm(19, (DEPTH, MLA_KV_RANK, MLA_HEADS * (MLA_NOPE + MLA_V)), MLA_KV_RANK ** -0.5),
        'gqa_q_norm': gain(20, (DEPTH, GQA_HD)),
        'gqa_k_norm': gain(21, (DEPTH, GQA_HD)),
        'diff_lq1': nrm(22, (DEPTH, DIFF_HD), 0.1),
        'diff_lk1': nrm(23, (DEPTH, DIFF_HD), 0.1),
        'diff_lq2': nrm(24, (DEPTH, DIFF_HD), 0.1),
        'diff_lk2': nrm(25, (DEPTH, DIFF_HD), 0.1),
        'diff_subln': gain(26, (DEPTH, DIFF_VD)),
        'hy_conv_w': nrm(27, (DEPTH, HY_CONV, 3 * HY_W), HY_CONV ** -0.5),
        'hy_conv_b': nrm(28, (DEPTH, 3 * HY_W), 0.02),
        'hy_fw1': nrm(29, (DEPTH, HY_EMB, HY_FFN), HY_EMB ** -0.5),
        'hy_fb1': nrm(30, (DEPTH, HY_FFN), 0.02),
        'hy_fw2': nrm(31, (DEPTH, HY_FFN, HY_FFN), HY_FFN ** -0.5),
        'hy_fb2': nrm(32, (DEPTH, HY_FFN), 0.02),
        'hy_fw3': nrm(33, (DEPTH, HY_FFN, HY_ORDER * 2 * HY_W), 0.1 * HY_FFN ** -0.5),
        'hy_freq': gain(34, (DEPTH, 2, HY_FFN)),
        'hy_decay': decay,
        'hy_bias': nrm(36, (DEPTH, HY_ORDER, HY_W), 0.5),
    }

def reference(x_prompt, x_sample, cache_mla_ckv, cache_mla_krope, cache_gqa_k, cache_gqa_v,
              cache_diff_k, cache_diff_v, c, c_ctx, norm_pre, norm_post, ada_w, ada_b, w_in, w_out,
              mla_q_norm, mla_wq_b, mla_kv_norm, mla_wkv_b, gqa_q_norm, gqa_k_norm,
              diff_lq1, diff_lk1, diff_lq2, diff_lk2, diff_subln, hy_conv_w, hy_conv_b,
              hy_fw1, hy_fb1, hy_fw2, hy_fb2, hy_fw3, hy_freq, hy_decay, hy_bias):
    y_prompt = x_prompt
    y_sample = x_sample
    s_ckv, s_kr, s_gk, s_gv, s_dk, s_dv = [], [], [], [], [], []
    for i in range(DEPTH):
        lp = dict(norm_pre=norm_pre[i], norm_post=norm_post[i], w_in=w_in[i], w_out=w_out[i],
                  mla_q_norm=mla_q_norm[i], mla_wq_b=mla_wq_b[i], mla_kv_norm=mla_kv_norm[i],
                  mla_wkv_b=mla_wkv_b[i], gqa_q_norm=gqa_q_norm[i], gqa_k_norm=gqa_k_norm[i],
                  diff_lq1=diff_lq1[i], diff_lk1=diff_lk1[i], diff_lq2=diff_lq2[i], diff_lk2=diff_lk2[i],
                  diff_subln=diff_subln[i], hy_conv_w=hy_conv_w[i], hy_conv_b=hy_conv_b[i],
                  hy_fw1=hy_fw1[i], hy_fb1=hy_fb1[i], hy_fw2=hy_fw2[i], hy_fb2=hy_fb2[i],
                  hy_fw3=hy_fw3[i], hy_freq=hy_freq[i], hy_decay=hy_decay[i], hy_bias=hy_bias[i])
        mod_ctx = (jax.nn.silu(c_ctx) @ ada_w[i] + ada_b[i])[None, :]
        mod_lat = jax.nn.silu(c) @ ada_w[i] + ada_b[i]
        y_prompt, st = trunk_layer(y_prompt, mod_ctx, lp, i, None)
        s_ckv.append(st[0]); s_kr.append(st[1]); s_gk.append(st[2])
        s_gv.append(st[3]); s_dk.append(st[4]); s_dv.append(st[5])
        ctx = (cache_mla_ckv[:, i], cache_mla_krope[:, i], cache_gqa_k[:, i], cache_gqa_v[:, i],
               cache_diff_k[:, i], cache_diff_v[:, i])
        y_sample, _ = trunk_layer(y_sample, mod_lat, lp, i, ctx)
    new_mla_ckv = jnp.stack(s_ckv, axis=1)
    new_mla_krope = jnp.stack(s_kr, axis=1)
    new_gqa_k = jnp.stack(s_gk, axis=1)
    new_gqa_v = jnp.stack(s_gv, axis=1)
    new_diff_k = jnp.stack(s_dk, axis=1)
    new_diff_v = jnp.stack(s_dv, axis=1)
    return (y_prompt, y_sample, new_mla_ckv, new_mla_krope, new_gqa_k, new_gqa_v, new_diff_k, new_diff_v)


_drawn_inputs = setup_inputs


def setup_inputs(seed=0):
    import zlib

    import numpy as np

    out = dict(_drawn_inputs(seed))
    spreads = {}
    factors = {'cache_mla_ckv': 8.0,
     'cache_mla_krope': 8.0,
     'cache_gqa_k': 8.0,
     'cache_gqa_v': 8.0,
     'cache_diff_k': 6.742,
     'cache_diff_v': 6.458,
     'mla_q_norm': 6.889,
     'gqa_q_norm': 7.55,
     'diff_lq1': 8.0,
     'diff_lk1': 8.0,
     'diff_lq2': 8.0,
     'diff_lk2': 8.0}
    for name, (base, spread) in spreads.items():
        noise = np.random.default_rng([zlib.crc32(name.encode()), seed]).standard_normal(out[name].shape)
        drawn = base * np.exp(spread * noise) if base else spread * noise
        out[name] = __import__('jax').numpy.asarray(drawn.astype(out[name].dtype))
    for name, factor in factors.items():
        out[name] = (out[name] * factor).astype(out[name].dtype)
    return out
```

```python
import math
from contextlib import ExitStack

import concourse.bass as bass
import numpy as np
from concourse import mybir

F32 = mybir.dt.float32
ACT = mybir.ActivationFunctionType
ALU = mybir.AluOpType
AX = mybir.AxisListType

P = 128
D = 1024
KD = D // P
DEPTH = 2
NT = 8
TT = NT + 1
TOK = TT * P
CACHE, PROMPT = NT, NT + 1
NKEY = NT + 2
GW = 256
EPS = 1e-6
WC = 512
CHUNKS = {"hy0": (2464, 512), "hy1": (2976, 512), "mla": (0, 416), "mla_gate": (416, 256),
          "gqa": (672, 512), "gqa_gate": (1184, 256), "diff": (1440, 512), "diff_vg": (1952, 512)}
STREAM = [("ada", j) for j in range(6)] + [(c, 0) for c in CHUNKS] + [("out", 0), ("out", 1)]
SLOT = {c: n % 2 for n, c in enumerate(STREAM)}
LAST_JOB = {**{("ada", j): ("ada", j) for j in range(6)},
            ("hy0", 0): ("u", 3, 2), ("hy1", 0): ("gate", "hy", NT),
            ("mla", 0): ("proj", "mla", NT), ("mla_gate", 0): ("gate", "mla", NT),
            ("gqa", 0): ("proj", "gqa", NT), ("gqa_gate", 0): ("gate", "gqa", NT),
            ("diff", 0): ("proj", "diff", NT), ("diff_vg", 0): ("gate", "diff", NT)}
PARTS = ((0, 512), (512, 512), (1024, 128))
TWO_PI = 2.0 * math.pi
PI_A = 6.28125
PI_B = math.floor((TWO_PI - PI_A) * 2 ** 23) / 2 ** 23
PI_C = TWO_PI - PI_A - PI_B
MAGIC = 12582912.0
PI_SAFE = 3.1415925
N_SAMPLE, N_PROMPT = NT * P, P

HT = 0
W0 = HT + KD * TOK
OT = W0 + 2 * KD * WC
FREE = OT + KD * TOK
A_MOD, A_ADAB, A_NPOST, A_FW3, A_FW = HT, HT + 3072, HT + 6144, HT + 7168, HT + 8192
A_HBIAS, A_DECAY = HT + 8320, HT + 8832
A_DEC = HT
EO = OT
TF = FREE
TI = TF + 4096
SGH = TI + 4096
HS = SGH + TT * GW
B2 = HS + 4608
B3 = B2 + 4608
HY_END = B3 + 4608
XV = OT
F_FEAT, F_ARG, F_K = TI, TI + TOK, TI + 2 * TOK
U0 = B2
UW = 10 * P + 130
CU = U0 + 2 * UW
ROPE = FREE
QT = ROPE + NT * 192
KT = QT + 4 * TOK
VV = KT + 4 * NKEY * P
SG = VV + NKEY * GW
PB = SG + TT * GW
PT = PB + 3 * TOK
OB = PT + 2 * TOK
ZB = OB + 2 * GW
WQB = ZB + 2 * WC
WKVB = WQB + 768
CT = WKVB + 512
QS = CT + 384
ATT_END = QS + 768
ROT, SQ, AUX = PB, PB + 1024, PB + 2048
KVGAIN, CKEY, CROPE, CKVOUT = AUX, AUX + 128, AUX + 384, AUX + 416
XN = B2
XR, GR, YN = FREE, FREE + 3 * D, FREE + 5 * D
NARENA = max(ATT_END, HY_END)
STAGES = ["ada", "filter", "norm", "hyena_in", "hyena", "mla", "gqa", "diff", "out"]
GROUPS = ("mla", "gqa", "diff")
NMAPS = {"mla": 1, "gqa": 1, "diff": 2}
DK = {"mla": 96, "gqa": 64, "diff": 32}
NH = 4
UNITS = [(t, h) for t in range(TT) for h in range(NH)]
NU = len(UNITS)
N_CONST = 5


def head(grp, h, s):
    if grp == "mla":
        return 0, h, h, 64 * h
    if grp == "gqa":
        return 64 * (h // 2), h % 2, 0, 64 * (h // 2)
    j = 2 * h + s
    return 32 * (j % 4), j // 4, j // 4, 64 * h


def key_tile(t):
    return PROMPT if t == NT else t


def n_keys(t):
    return 1 if t == NT else NT + 1


class Signals:

    ONCE = ("constants", "x_copied", "silu_ready", "exponent_set", "layer_finished", "semaphores_cleared", "layer_entered")

    def __init__(self, nc, ctx, known):
        self.nc, self.ctx, self.known = nc, ctx, known
        self.sem, self.count, self.mark = {}, {}, {}
        for name in self.ONCE:
            self.raw(name)
        for name in (known[0] if known else ()):
            self.raw(name)

    def raw(self, name):
        if name not in self.sem:
            self.sem[name] = self.ctx.enter_context(self.nc.semaphore(name))
            self.count[name] = 0
        return self.sem[name]

    def counted_by_layer(self):
        numbers = [s.num for n, s in self.sem.items() if n not in self.ONCE]
        assert not self.known or sorted(numbers) == list(range(min(numbers), max(numbers) + 1))
        return range(min(numbers), max(numbers) + 1)

    def up(self, name, key=None, n=1):
        s = self.raw(name)
        self.count[name] += n
        self.mark[name, key] = self.count[name]
        return s, n

    def now(self, name):
        return self.raw(name), self.count[name]

    def at(self, name, key=None):
        return self.raw(name), (self.known[1][name, key] if self.known else 1)

    def all(self, name):
        return self.raw(name), (self.known[0][name] if self.known else 1)


class Banks:

    def __init__(self, signals, known):
        self.s, self.known = signals, known
        self.filled, self.drains, self.last, self.jobs = {}, {}, {}, {}
        self.turn = 0

    def next(self):
        self.turn += 1
        return [self.turn % 8]

    def claim(self, job, banks, drains=1):
        found = {self.last[b] for b in banks if b in self.last}
        b0 = banks[0]
        self.filled[b0] = self.filled.get(b0, 0) + 1
        self.drains[b0] = self.drains.get(b0, 0) + drains
        for b in banks:
            self.last[b] = (b0, self.drains[b0])
        assert job not in self.jobs, job
        self.jobs[job] = (b0, self.filled[b0], self.drains[b0])
        return [(self.s.raw(f"bank{b}_drained"), v) for b, v in sorted(found)]

    def bank(self, job):
        return self.known[2][job][0] if self.known else 0

    def done(self, job):
        return self.s.up(f"bank{self.jobs[job][0]}_filled", job)

    def full(self, job):
        return self.s.raw(f"bank{self.bank(job)}_filled"), (self.known[2][job][1] if self.known else 1)

    def drained(self, job):
        return self.s.up(f"bank{self.bank(job)}_drained", job)

    def emptied(self, job):
        return self.s.raw(f"bank{self.bank(job)}_drained"), (self.known[2][job][2] if self.known else 1)


def program(nc, I, outs, known=None):
    with ExitStack() as ctx:
        ctx.enter_context(nc.allow_non_contiguous_dma(reason="a few short parameter columns"))
        S = Signals(nc, ctx, known)
        K = Banks(S, known)

        def sb(name, shape):
            return ctx.enter_context(nc.sbuf_tensor(name, shape, F32))

        R = sb("arena", [P, NARENA])

        def at(off, *shape, parts=P, base=0):
            v = R[base:base + parts, off:off + int(np.prod(shape))]
            if len(shape) == 1:
                return v
            g = "abcd"[:len(shape)]
            return v.rearrange(f"p ({' '.join(g)}) -> p {' '.join(g)}", **dict(zip(g, shape)))

        ident = sb("ident", [P, P])
        sel = sb("sel", [2, 2, P])
        csil = sb("csil", [P, KD, 2])
        craw = sb("craw", [P, KD, 2])
        mcol = sb("mcol", [P, 2 * KD, 2])
        gpre = sb("gpre", [P, KD])
        negt = sb("negt", [P, TT])
        st = sb("st", [P, 80])
        lamv = sb("lamv", [P, 8])
        mhalf = sb("mhalf", [P, 8])
        mg = sb("mg", [P, 3])
        fwp = sb("fwp", [64, 4])
        hcw = sb("hcw", [P, 6, 4])
        psum = ctx.enter_context(nc.psum_tensor("psum", [P, 8 * 512], F32))
        bank = [psum[:, 512 * i:512 * (i + 1)] for i in range(8)]

        def score_view(group, n):
            return psum[:, 1536 * group:1536 * group + n]

        def B(job, n=512, parts=P):
            return bank[K.bank(job)][0:parts, 0:n]

        hT = at(HT, KD, TOK)
        oT = at(OT, KD, TOK)
        W = at(W0, 2, KD, WC)
        xs, spectrum_kept, gates_kept = outs["xs"], outs["spectrum_kept"], outs["gates_kept"]

        def rows(t):
            return slice(t, NT * P, NT) if t < NT else slice(NT * P, TOK)

        def stage_value(k):
            return S.raw("stage_done"), 4 * k

        passed = {}

        def stage_end(eng):
            eng.drain().then_inc(S.raw("stage_done"), 1)
            passed[id(eng)] = passed.get(id(eng), 0) + 1
            eng.wait_ge(*stage_value(passed[id(eng)]))

        def layer_end(eng):
            eng.drain().then_inc(S.raw("layer_finished"), 1)
            eng.wait_ge(S.raw("semaphores_cleared"), 1)
            eng.sem_inc(S.raw("layer_entered"), 1)

        block = ctx.enter_context(nc.Block())

        @block.sync
        def _(sp):
            def load(dst, src, name, key=None):
                sp.dma_start(dst, src).then_inc(*S.up(name, key, 16))

            sp.dma_start(ident[:, :], I["ident"]).then_inc(S.raw("constants"), 16)
            sp.dma_start(sel[:, :, :], I["sel"]).then_inc(S.raw("constants"), 16)
            sp.dma_start(craw[:, :, 0:1], I["c"].rearrange("o (k p) -> p k o", p=P)).then_inc(S.raw("constants"), 16)
            sp.dma_start(craw[:, :, 1:2], I["c_ctx"].rearrange("(o k p) -> p k o", p=P, o=1)).then_inc(S.raw("constants"), 16)
            sp.dma_start(negt[:, :], I["negt"]).then_inc(S.raw("constants"), 16)
            sp.dma_start(xs[0], I["x"]).then_inc(S.raw("x_copied"), 16)
            with sp.Fori(0, DEPTH) as l:
                def lay(name):
                    return I[name][bass.ds(l, 1)]

                def row(name, n=P):
                    return lay(name).to_broadcast([n, lay(name).shape[1]])

                turn = [0]

                def chunk():
                    name, j = c = STREAM[turn[0]]
                    if turn[0] >= 2:
                        sp.wait_ge(*K.full(LAST_JOB[STREAM[turn[0] - 2]]))
                    turn[0] += 1
                    if name in ("ada", "out"):
                        src, n = lay("ada_w" if name == "ada" else "w_out")[:, :, j * WC:(j + 1) * WC], WC
                    else:
                        c0, n = CHUNKS[name]
                        src = lay("w_in")[:, :, c0:c0 + n]
                    load(W[:, SLOT[c], :, 0:n], src.rearrange("o (k p) n -> p (o k) n", p=P),
                         f"weights{SLOT[c]}_loaded", c)

                sp.wait_ge(S.raw("x_copied"), 16)
                chunk()
                chunk()
                for s in range(2):
                    load(at(A_ADAB, 3072, parts=1, base=s), lay("ada_b"), "ada_params")
                load(at(A_NPOST, D), row("norm_post"), "ada_params")
                load(gpre[:, :], lay("norm_pre").rearrange("o (k p) -> p (o k)", p=P), "ada_params")
                load(at(A_FW, 64, parts=33), lay("hy_fw1").rearrange("o k n -> (o k) n"), "filter_params")
                load(at(A_FW + 64, 64, parts=64), lay("hy_fw2").rearrange("o k n -> (o k) n"), "filter_params")
                load(at(A_FW3, 1024, parts=64), lay("hy_fw3").rearrange("o k n -> (o k) n"), "filter_params")
                load(fwp[:, 0:1], lay("hy_fb1").rearrange("o k -> k o"), "filter_params")
                load(fwp[:, 1:2], lay("hy_fb2").rearrange("o k -> k o"), "filter_params")
                load(fwp[:, 2:4], lay("hy_freq").rearrange("o f k -> k (o f)"), "filter_params")
                load(at(A_HBIAS, 512), row("hy_bias2"), "filter_params")
                load(at(A_DECAY, GW), row("hy_decay"), "filter_params")
                load(at(F_FEAT, TOK, parts=33), I["feats"], "filter_params")
                load(at(TF, 4096), I["tab_f"], "filter_params")
                for f in range(6):
                    load(hcw[:, f, 0:3], lay("hy_conv_w")[:, :, f * P:(f + 1) * P].rearrange("o t p -> p (o t)"), "conv_params")
                load(hcw[:, :, 3:4], lay("hy_conv_b").rearrange("o (f p) -> p f o", p=P), "conv_params")
                load(mg[:, 0:2], lay("mla_q_norm").rearrange("o (k p) -> p (o k)", p=P), "mla_gains")
                load(mg[:, 2:3], lay("mla_kv_norm").rearrange("o p -> p o"), "mla_gains")
                for _ in range(4):
                    chunk()
                sp.wait_ge(*stage_value(1))
                sp.dma_start(gates_kept, at(SGH, 2 * D)).then_inc(*S.up("gate_rows_kept", None, 16))
                chunk()
                chunk()
                sp.wait_ge(*S.at("butterfly_pool", ("F", 1)))
                sp.wait_ge(*S.at("spectrum1_made"))
                sp.dma_start(spectrum_kept, at(HS, 4608)).then_inc(*S.up("spectrum1_kept", None, 16))
                sp.wait_ge(*stage_value(2))
                for t in range(TT):
                    if t >= 2:
                        sp.wait_ge(*K.full(("xT", t - 2, 1)))
                    load(at(XN + (t % 2) * D, D), xs[bass.ds(l, 1)][:, rows(t), :].rearrange("o p n -> (o p) n"),
                         f"x{t % 2}_loaded", t)
                load(at(TI, 4096), I["tab_i"], "inverse_table")
                chunk()
                chunk()
                sp.wait_ge(*S.at("product_vector", 0))
                sp.wait_ge(*S.at("product_pool", 0))
                sp.wait_ge(*S.at("spectrum1_kept"))
                load(at(HS, 4608), spectrum_kept, "spectrum1_back")
                sp.wait_ge(*stage_value(5))
                load(at(ROPE, NT, 192), I["rope"], "mla_params")
                load(at(WQB, 2, 384), lay("mla_wq_b").rearrange("o (k p) n -> p (o k) n", p=P), "mla_params")
                load(at(WKVB, 512), lay("mla_wkv_b").rearrange("o p n -> (o p) n"), "mla_params")
                load(at(KVGAIN, P), row("mla_kv_norm"), "mla_params")
                load(at(CKEY, P), I["cache_mla_ckv"][0][bass.ds(l, 1)].rearrange("o p n -> (o p) n"), "mla_params")
                load(at(CROPE, 32), I["cache_mla_krope"][0][bass.ds(l, 1)].rearrange("o p n -> (o p) n"), "mla_params")
                sp.wait_ge(*S.at("state_ready", "mla"))
                sp.dma_start(outs["new_mla_ckv"][0][bass.ds(l, 1)].rearrange("o p n -> (o p) n"),
                             at(CKVOUT, P)).then_inc(*S.up("state_stored", ("mla", 0), 16))
                sp.dma_start(outs["new_mla_krope"][0][bass.ds(l, 1)].rearrange("o p n -> (o p) n"),
                             at(ZB + 384, 32)).then_inc(*S.up("state_stored", "mla", 16))
                chunk()
                chunk()
                sp.wait_ge(*stage_value(6))
                for h in range(4):
                    load(at(WQB + 64 * h, 64), row("gqa_q_norm"), "gqa_params")
                for h in range(2):
                    load(at(WQB + 256 + 64 * h, 64), row("gqa_k_norm"), "gqa_params")
                load(at(CKEY, P), I["cache_gqa_k"][0][bass.ds(l, 1)].rearrange("o p h n -> (o p) (h n)"), "gqa_params")
                load(at(VV + CACHE * GW, P), I["cache_gqa_v"][0][bass.ds(l, 1)].rearrange("o p h n -> (o p) (h n)"), "gqa_params")
                sp.wait_ge(*S.at("state_ready", "gqa"))
                sp.wait_ge(*K.emptied(("proj", "gqa", NT)))
                sp.dma_start(outs["new_gqa_k"][0][bass.ds(l, 1)].rearrange("o p h n -> (o p) (h n)"),
                             at(ZB + 256, P)).then_inc(*S.up("state_stored", ("gqa", 0), 16))
                sp.dma_start(outs["new_gqa_v"][0][bass.ds(l, 1)].rearrange("o p h n -> (o p) (h n)"),
                             at(VV + PROMPT * GW, P)).then_inc(*S.up("state_stored", "gqa", 16))
                chunk()
                chunk()
                sp.wait_ge(*stage_value(7))
                load(at(WQB, 64), row("diff_subln"), "diff_params")
                for i, v in enumerate(("diff_lq1", "diff_lk1", "diff_lq2", "diff_lk2")):
                    load(at(WQB + 64 + 32 * i, 32), row(v), "diff_params")
                load(lamv[:, 4:6], row("lam_init"), "diff_params")
                load(at(CKEY, GW), I["cache_diff_k"][0][bass.ds(l, 1)].rearrange("o p h n -> (o p) (h n)"), "diff_params")
                load(at(VV + CACHE * GW, GW), I["cache_diff_v"][0][bass.ds(l, 1)].rearrange("o p h n -> (o p) (h n)"), "diff_params")
                sp.wait_ge(*K.emptied(("proj", "diff", NT)))
                sp.dma_start(outs["new_diff_k"][0][bass.ds(l, 1)].rearrange("o p h n -> (o p) (h n)"),
                             at(ZB + 256, GW)).then_inc(*S.up("state_stored", ("diff", 0), 16))
                sp.wait_ge(*K.emptied(("gate", "diff", NT)))
                sp.dma_start(outs["new_diff_v"][0][bass.ds(l, 1)].rearrange("o p h n -> (o p) (h n)"),
                             at(VV + PROMPT * GW, GW)).then_inc(*S.up("state_stored", "diff", 16))
                chunk()
                chunk()
                sp.wait_ge(*stage_value(8))
                load(at(GR, 2 * D), gates_kept, "gate_rows_back")

                def store_x(t):
                    sp.wait_ge(*S.at("x_updated", t))
                    sp.dma_start(xs[bass.ds(l + 1, 1)][:, rows(t), :].rearrange("o p n -> (o p) n"),
                                 at(XR + (t % 3) * D, D)).then_inc(*S.up(f"x_stored{t % 3}", t, 16))

                for t in range(TT):
                    if t >= 3:
                        store_x(t - 3)
                        sp.wait_ge(*S.at(f"x_stored{t % 3}", t - 3))
                    load(at(XR + (t % 3) * D, D), xs[bass.ds(l, 1)][:, rows(t), :].rearrange("o p n -> (o p) n"),
                         f"xr{t % 3}_loaded", t)
                for t in range(TT - 3, TT):
                    store_x(t)
                for name in ("x_stored0", "x_stored1", "x_stored2", "state_stored"):
                    sp.wait_ge(*S.all(name))
                sp.wait_ge(S.raw("layer_finished"), 4)
                sp.sem_clear(S.counted_by_layer())
                sp.sem_clear(S.raw("layer_finished"))
                sp.sem_inc(S.raw("semaphores_cleared"), 1)
                sp.wait_ge(S.raw("layer_entered"), 4)
                sp.sem_clear(S.raw("semaphores_cleared"))
                sp.sem_clear(S.raw("layer_entered"))

        @block.tensor
        def _(pe):
            def claim(job, banks, drains=1):
                for w in K.claim(job, banks, drains):
                    pe.wait_ge(*w)
                return bank[banks[0]]

            def mm(out, lhsT, rhs, start=True, stop=True):
                return nc.tensor.matmul(out, lhsT, rhs, start=start, stop=stop)

            def flip(out, src):
                n = src.shape[0]
                return nc.tensor.transpose(out, src, ident[0:n, 0:n])

            pe.wait_ge(S.raw("constants"), 16 * N_CONST)
            pe.wait_ge(S.raw("silu_ready"), 3)
            with pe.Fori(0, DEPTH) as l:
                def weights(c, j=0):
                    pe.wait_ge(*S.at(f"weights{SLOT[c, j]}_loaded", (c, j)))

                for j in range(6):
                    weights("ada", j)
                    ps = claim(("ada", j), [j])
                    for k in range(KD):
                        last = mm(ps[0:2, :], csil[:, k, :], W[:, j % 2, k, :], k == 0, k == KD - 1)
                    last.then_inc(*K.done(("ada", j)))
                mod = at(A_MOD, 3072, parts=2)
                for j in range(4):
                    pe.wait_ge(*K.emptied(("ada", j)))
                ps = claim(("modT",), [6])
                for m in range(2 * KD):
                    last = flip(ps[:, 2 * m:2 * m + 2], mod[:, m * P:(m + 1) * P])
                last.then_inc(*K.done(("modT",)))
                for s in range(2):
                    for half in range(2):
                        pe.wait_ge(*K.emptied(("ada", 4 + half)))
                        ps = claim(("gate_row", s, half), [2 * s + half])
                        mm(ps[:, :], sel[:, s, :], mod[:, 2 * D + half * 512:2 * D + (half + 1) * 512]
                           ).then_inc(*K.done(("gate_row", s, half)))
                stage_end(pe)

                pe.wait_ge(*S.at("filter_params"))
                for i, (c, n) in enumerate(PARTS):
                    ps = claim(("f1", i), K.next())
                    mm(ps[0:64, 0:n], at(A_FW, 64, parts=33), at(F_FEAT + c, n, parts=33)
                       ).then_inc(*K.done(("f1", i)))
                pe.wait_ge(*S.at("sine", 1))
                for i, (c, n) in enumerate(PARTS):
                    ps = claim(("f2", i), K.next())
                    mm(ps[0:64, 0:n], at(A_FW + 64, 64, parts=64), at(F_ARG + c, n, parts=64)
                       ).then_inc(*K.done(("f2", i)))
                pe.wait_ge(*S.at("sine", 2))
                tf = at(TF, 2 * NT, 2, P)
                ti = at(TI, 2 * NT, 2, P)
                eo = at(EO, TT, 3, GW)
                for o in (1, 0):
                    for t in range(TT):
                        ps = claim(("f3", o, t), K.next())
                        mm(ps[:, :], at(F_ARG + t * P, P, parts=64), at(A_FW3 + o * 512, 512, parts=64)
                           ).then_inc(*K.done(("f3", o, t)))
                    pe.wait_ge(*S.at("filter_negated", o))
                    for a0 in range(4):
                        back = (4 - a0) % 4
                        for p in range(2):
                            ps = claim(("FE", o, a0, p), K.next())
                            for ri in range(2):
                                terms = [(a, 0) for a in (a0, a0 + 4)] + [(a, 1 + ri) for a in (back, back + 4)]
                                for i, (a, kind) in enumerate(terms):
                                    last = mm(ps[:, ri * GW:(ri + 1) * GW], tf[:, 2 * a + p, ri, :],
                                              eo[:, a, kind, :], i == 0, i == 3)
                            last.then_inc(*K.done(("FE", o, a0, p)))
                    ps = claim(("FEp", o), K.next())
                    for ri in range(2):
                        for i, kind in enumerate((0, 1 + ri)):
                            last = mm(ps[:, ri * GW:(ri + 1) * GW], tf[:, 0, ri, :], eo[:, NT, kind, :], i == 0, i == 1)
                    last.then_inc(*K.done(("FEp", o)))
                stage_end(pe)

                for t in range(TT):
                    pe.wait_ge(*S.at("x_normed", t))
                    for half in range(2):
                        ps = claim(("xT", t, half), K.next())
                        for k in range(4):
                            last = flip(ps[:, k * P:(k + 1) * P], at(XN + (t % 2) * D + (half * 4 + k) * P, P))
                        last.then_inc(*K.done(("xT", t, half)))
                stage_end(pe)

                def to_tokens(f):
                    for g in range(3):
                        if g == 0:
                            pe.wait_ge(*S.at("taps", f))
                        ps = claim(("uT", f, g), K.next())
                        for i in range(1 if g == 2 else 4):
                            last = flip(ps[:, i * P:(i + 1) * P], at(CU + (f % 2) * TOK + (4 * g + i) * P, P))
                        last.then_inc(*K.done(("uT", f, g)))

                for f in range(6):
                    c = "hy0" if f < 4 else "hy1"
                    weights(c)
                    for i, (tok, n) in enumerate(PARTS):
                        ps = claim(("u", f, i), K.next())
                        for k in range(KD):
                            last = mm(ps[:, 0:n], W[:, SLOT[c, 0], k, (f % 4) * P:(f % 4 + 1) * P],
                                      hT[:, k, tok:tok + n], k == 0, k == KD - 1)
                        last.then_inc(*K.done(("u", f, i)))
                    if f >= 1:
                        to_tokens(f - 1)

                def project(grp, kind, t, c, c0, n, drains=1):
                    job = (kind, grp, t)
                    ps = claim(job, K.next(), drains)
                    for k in range(KD):
                        last = mm(ps[:, 0:n], hT[:, k, t * P:(t + 1) * P], W[:, SLOT[c, 0], k, c0:c0 + n],
                                  k == 0, k == KD - 1)
                    last.then_inc(*K.done(job))

                for t in range(TT):
                    project("hy", "gate", t, "hy1", 256, GW)
                    if t == 1:
                        to_tokens(5)
                stage_end(pe)

                zv = at(XV, TT, 3, GW)
                for o in range(2):
                    for a0 in range(4):
                        if o == 1:
                            pe.wait_ge(*K.emptied(("Y", 0, a0 // 2)))
                            pe.wait_ge(*K.emptied(("Y", 0, 2 + a0 // 2)))
                        for p in range(2):
                            ps = claim(("Z", o, a0, p), K.next())
                            for ri in range(2):
                                for i, a in enumerate((a0, a0 + 4)):
                                    last = mm(ps[:, ri * GW:(ri + 1) * GW], tf[:, 2 * a + p, ri, :],
                                              zv[:, a, 2, :], i == 0, i == 1)
                            last.then_inc(*K.done(("Z", o, a0, p)))
                    if o == 1:
                        pe.wait_ge(*K.emptied(("Yp", 0)))
                    ps = claim(("Zp", o), K.next())
                    for ri in range(2):
                        last = mm(ps[:, ri * GW:(ri + 1) * GW], tf[:, 0, ri, :], zv[:, NT, 2, :])
                    last.then_inc(*K.done(("Zp", o)))
                    if o == 0:
                        pe.wait_ge(*S.at("inverse_table"))
                    pe.wait_ge(*S.at("butterfly_vector", ("G", o)))
                    pe.wait_ge(*S.at("butterfly_pool", ("G", o)))
                    G = at(B3, 4, 2, 2, GW)
                    for i in range(4):
                        ps = claim(("Y", o, i), K.next())
                        for a in (2 * i, 2 * i + 1):
                            terms = [(p, ri) for p in range(2) for ri in range(2)]
                            for n, (p, ri) in enumerate(terms):
                                last = mm(ps[:, (a % 2) * GW:(a % 2 + 1) * GW], ti[:, 2 * a + p, ri, :],
                                          G[:, a % 4, p, ri, :], n == 0, n == 3)
                        last.then_inc(*K.done(("Y", o, i)))
                    pe.wait_ge(*S.at("product_prompt", o))
                    ps = claim(("Yp", o), K.next())
                    for ri in range(2):
                        last = mm(ps[:, 0:GW], ti[:, 0, ri, :], at(B3 + 4096 + ri * GW, GW), ri == 0, ri == 1)
                    last.then_inc(*K.done(("Yp", o)))

                def out_tile(grp, t, src, banks):
                    pe.wait_ge(*S.at("gated", (grp, t)))
                    ps = claim(("oT", grp, t), banks)
                    for i in range(2):
                        last = flip(ps[:, i * P:(i + 1) * P], src[:, i * P:(i + 1) * P])
                    last.then_inc(*K.done(("oT", grp, t)))

                for t in range(TT):
                    out_tile("hy", t, zv[:, t, 2, :], K.next())
                stage_end(pe)

                def attention(grp):
                    dk = DK[grp]
                    two = NMAPS[grp] == 2

                    def scores(i):
                        t, h = UNITS[i]
                        for s in range(NMAPS[grp]):
                            g = s if two else i % 2
                            ps = claim(("S", grp, i, s), [3 * g, 3 * g + 1, 3 * g + 2])
                            base, qi, ki, _ = head(grp, h, s)
                            q = at(QT + qi * TOK + t * P, P, parts=dk, base=base)
                            k0 = ki * NKEY * P + (PROMPT * P if t == NT else 0)
                            for j, (c, n) in enumerate(((0, P),) if t == NT else PARTS):
                                last = mm(bank[3 * g + j][:, 0:n], q, at(KT + k0 + c, n, parts=dk, base=base))
                            last.then_inc(*K.done(("S", grp, i, s)))

                    def turn_one(i):
                        t, _ = UNITS[i]
                        pe.wait_ge(*K.emptied(("S", grp, i, 0)))
                        g = i % 2
                        claim(("T", grp, i), [3 * g, 3 * g + 1, 3 * g + 2], 1 if t == NT else 2)
                        for j in range(n_keys(t)):
                            last = flip(bank[3 * g + j // 4][:, (j % 4) * P:(j % 4 + 1) * P],
                                        at(PB + (i % 2) * TOK + j * P, P))
                        last.then_inc(*K.done(("T", grp, i)))

                    def turn_two(i):
                        t, _ = UNITS[i]
                        pe.wait_ge(*S.at("combined", i))
                        for b in range((n_keys(t) + 3) // 4):
                            ps = claim(("T", grp, i, b), [6])
                            for j in range(4 * b, min(4 * b + 4, n_keys(t))):
                                last = flip(ps[:, (j % 4) * P:(j % 4 + 1) * P], at(PB + (i % 2) * TOK + j * P, P))
                            last.then_inc(*K.done(("T", grp, i, b)))

                    def values(i):
                        t, h = UNITS[i]
                        _, _, _, vc = head(grp, h, 0)
                        ps = claim(("O", grp, i), [7 if two else 6])
                        nk = n_keys(t)
                        for j in range(nk):
                            if two and j % 4 == 0:
                                pe.wait_ge(*K.emptied(("T", grp, i, j // 4)))
                            elif j == 0:
                                pe.wait_ge(*K.emptied(("T", grp, i)))
                            kt = PROMPT if t == NT else j
                            last = mm(ps[:, 0:64], at(PT + (i % 2) * TOK + j * P, P),
                                      at(VV + kt * GW + vc, 64), j == 0, j == nk - 1)
                        last.then_inc(*K.done(("O", grp, i)))

                    lag = 1 if two else 2
                    for i in range(NU + lag + 1):
                        if i < NU:
                            scores(i)
                        if 1 <= i <= NU:
                            (turn_two if two else turn_one)(i - 1)
                        if lag <= i < NU + lag:
                            values(i - lag)
                        n = i - lag - 1
                        if n >= 0 and n % NH == NH - 1:
                            t = UNITS[n][0]
                            out_tile(grp, t, at(OB + (t % 2) * GW, GW), [7])

                def gates(grp, c):
                    weights(c)
                    for t in range(TT):
                        project(grp, "gate", t, c, 0, CHUNKS[c][1])

                def mla_latent(t):
                    pe.wait_ge(*S.at("latent", t))
                    ps = claim(("cT", t), K.next())
                    if t < TT:
                        for i in range(3):
                            last = flip(ps[:, i * P:(i + 1) * P], at(ZB + (t % 2) * WC + i * P, P))
                    else:
                        last = flip(ps[:, 2 * P:3 * P], at(CKEY, P))
                    last.then_inc(*K.done(("cT", t)))

                def mla_expand(t):
                    pe.wait_ge(*K.emptied(("cT", t)))
                    if t < TT:
                        ps = claim(("q", t), K.next())
                        for k in range(2):
                            last = mm(ps[:, 0:384], at(CT + k * P, P), at(WQB + k * 384, 384), k == 0, k == 1)
                        last.then_inc(*K.done(("q", t)))
                    ps = claim(("kv", t), K.next())
                    mm(ps[:, :], at(CT + 2 * P, P), at(WKVB, 512)).then_inc(*K.done(("kv", t)))

                def mla_turn(t):
                    if t < TT:
                        pe.wait_ge(*S.at("q_roped", t))
                        ps = claim(("qT", t), K.next())
                        for h in range(NH):
                            last = flip(ps[0:96, h * P:(h + 1) * P], at(QS + h * 96, 96))
                        last.then_inc(*K.done(("qT", t)))
                    pe.wait_ge(*K.emptied(("kv", t)))
                    pe.wait_ge(*S.at("k_rope_spread", t))
                    ps = claim(("kT", t), K.next())
                    for h in range(NH):
                        last = flip(ps[0:96, h * P:(h + 1) * P], at(QS + 384 + h * 96, 96))
                    last.then_inc(*K.done(("kT", t)))

                weights("mla")
                pe.wait_ge(*S.at("mla_params"))
                for i in range(TT + 3):
                    if 1 <= i <= TT + 1:
                        mla_latent(i - 1)
                    if i < TT:
                        project("mla", "proj", i, "mla", 0, 416)
                    if 2 <= i <= TT + 2:
                        mla_turn(i - 2)
                    if 1 <= i <= TT + 1:
                        mla_expand(i - 1)
                gates("mla", "mla_gate")
                pe.wait_ge(*K.emptied(("qT", NT)))
                pe.wait_ge(*K.emptied(("kT", TT)))
                attention("mla")
                stage_end(pe)

                for grp, nq, nk in (("gqa", 2, 1), ("diff", 2, 2)):
                    def turn_heads(t):
                        if t < TT:
                            pe.wait_ge(*S.at("heads_ready", (grp, t)))
                        ps = claim(("hT", grp, t), K.next())
                        if t < TT:
                            for i in range(nq + nk):
                                last = flip(ps[:, i * P:(i + 1) * P], at(ZB + (t % 2) * WC + i * P, P))
                        else:
                            for i in range(nk):
                                last = flip(ps[:, (nq + i) * P:(nq + i + 1) * P], at(CKEY + i * P, P))
                        last.then_inc(*K.done(("hT", grp, t)))

                    weights(grp)
                    pe.wait_ge(*S.at(f"{grp}_params"))
                    for i in range(TT + 1):
                        if i < TT:
                            project(grp, "proj", i, grp, 0, 512)
                        if i >= 1:
                            turn_heads(i - 1)
                    turn_heads(TT)
                    gates(grp, "gqa_gate" if grp == "gqa" else "diff_vg")
                    pe.wait_ge(*K.emptied(("hT", grp, NT)))
                    pe.wait_ge(*K.emptied(("hT", grp, TT)))
                    pe.wait_ge(*K.emptied(("gate", grp, NT)))
                    attention(grp)
                    stage_end(pe)

                for half in range(2):
                    weights("out", half)
                for t in range(TT):
                    for half in range(2):
                        ps = claim(("y", t, half), K.next())
                        for k in range(KD):
                            last = mm(ps[:, :], oT[:, k, t * P:(t + 1) * P], W[:, half, k, :], k == 0, k == KD - 1)
                        last.then_inc(*K.done(("y", t, half)))
                stage_end(pe)
                layer_end(pe)

        @block.scalar
        def _(act):
            def link(ins):
                ins.then_inc(*S.up("scalar_step"))
                act.wait_ge(*S.now("scalar_step"))

            act.wait_ge(S.raw("constants"), 16 * N_CONST)
            nc.scalar.activation(csil[:, :, :], craw[:, :, :], ACT.Tanh, scale=0.5).then_inc(S.raw("silu_ready"), 1)
            with act.Fori(0, DEPTH) as l:
                stage_end(act)

                act.wait_ge(*S.at("filter_params"))
                link(nc.scalar.activation(at(A_DECAY, GW), at(A_DECAY, GW), ACT.Abs))
                for t in range(TT):
                    nc.scalar.activation(at(A_DEC + t * GW, GW), at(A_DECAY, GW), ACT.Exp, scale=negt[:, t:t + 1]
                                         ).then_inc(*S.up("decay", t))
                for n in (1, 2):
                    act.wait_ge(*S.at("angle", n))
                    nc.scalar.activation(at(F_ARG, TOK, parts=64), at(F_ARG, TOK, parts=64), ACT.Sin
                                         ).then_inc(*S.up("sine", n))
                for o in (1, 0):
                    if o == 0:
                        act.wait_ge(*S.at("butterfly_sums", ("F", 1)))
                        act.wait_ge(*S.at("butterfly_diffs", ("F", 1)))
                        act.wait_ge(*S.at("spectrum1_made"))
                    for a0 in range(4):
                        for p in range(2):
                            job = ("FE", o, a0, p)
                            act.wait_ge(*K.full(job))
                            nc.scalar.mul(at(B2 + (a0 * 2 + p) * 512, 512), B(job), 1.0 / N_SAMPLE
                                          ).then_inc(*K.drained(job))
                    act.wait_ge(*K.full(("FEp", o)))
                    nc.scalar.mul(at(B2 + 4096, 512), B(("FEp", o)), 1.0 / N_PROMPT).then_inc(*K.drained(("FEp", o)))
                stage_end(act)

                for t in range(TT + 1):
                    if t < TT:
                        act.wait_ge(*S.at(f"x{t % 2}_loaded", t))
                        if t >= 1:
                            act.wait_ge(*S.at("x_squares", t - 1))
                        nc.scalar.activation(at(B3, D), at(XN + (t % 2) * D, D), ACT.Square,
                                             accum_out=st[:, t:t + 1]).then_inc(*S.up("x_squares", t))
                    if t >= 1:
                        job, s = ("xT", t - 1, 0), int(t - 1 == NT)
                        act.wait_ge(*K.full(job))
                        for k in range(4):
                            last = nc.scalar.activation(hT[:, k, (t - 1) * P:t * P], B(job)[:, k * P:(k + 1) * P],
                                                        ACT.Identity, scale=mcol[:, KD + k, s:s + 1],
                                                        bias=mcol[:, k, s:s + 1])
                        last.then_inc(*K.drained(job))
                stage_end(act)

                act.wait_ge(*S.at("conv_params"))
                for f in range(6):
                    u = U0 + (f % 2) * UW
                    if f >= 2:
                        act.wait_ge(*S.at("taps", f - 2))
                    for i in range(3):
                        job = ("u", f, i)
                        act.wait_ge(*K.full(job))
                        dst = at(u + (1 + 4 * i) * P, 512) if i < 2 else at(u + 10 * P + 1, P)
                        nc.scalar.copy(dst, B(job, 512 if i < 2 else P)).then_inc(*K.drained(job))
                        act.wait_ge(*K.emptied(job))
                    if f >= 2:
                        act.wait_ge(*K.full(("uT", f - 2, 2)))
                    nc.scalar.activation(at(CU + (f % 2) * TOK, D), at(u + P, D), ACT.Identity,
                                         scale=hcw[:, f, 1:2], bias=hcw[:, f, 3:4])
                    nc.scalar.activation(at(CU + (f % 2) * TOK + D, P), at(u + 10 * P + 1, P), ACT.Identity,
                                         scale=hcw[:, f, 1:2], bias=hcw[:, f, 3:4]).then_inc(*S.up("middle_tap", f))
                    if f >= 1:
                        drain_uT = f - 1
                        for g in (0,):
                            job = ("uT", drain_uT, g)
                            act.wait_ge(*K.full(job))
                            nc.scalar.copy(at(XV, TT, 768)[:, 0:4, drain_uT * P:(drain_uT + 1) * P],
                                           B(job).rearrange("p (a n) -> p a n", a=4)).then_inc(*K.drained(job))
                def half_tanh(grp, t, c0=0):
                    job = ("gate", grp, t)
                    act.wait_ge(*K.full(job))
                    if t >= 2:
                        act.wait_ge(*K.emptied(("gate", grp, t - 2)))
                    dst = (CU + 2 * TOK if grp == "hy" else OB) + (t % 2) * GW
                    nc.scalar.activation(at(dst, GW), B(job)[:, c0:c0 + GW], ACT.Tanh, scale=0.5
                                         ).then_inc(*S.up("half_tanh", (grp, t)))

                for t in range(TT):
                    half_tanh("hy", t)
                    if t == 1:
                        job = ("uT", 5, 0)
                        act.wait_ge(*K.full(job))
                        nc.scalar.copy(at(XV, TT, 768)[:, 0:4, 5 * P:6 * P],
                                       B(job).rearrange("p (a n) -> p a n", a=4)).then_inc(*K.drained(job))
                stage_end(act)

                for o in range(2):
                    if o == 1:
                        act.wait_ge(*K.full(("Y", 0, 3)))
                    for a0 in range(4):
                        job = ("Z", o, a0, 0)
                        act.wait_ge(*K.full(job))
                        nc.scalar.copy(at(B2 + (a0 * 2) * 512, 512), B(job)).then_inc(*K.drained(job))
                    act.wait_ge(*K.full(("Zp", o)))
                    nc.scalar.copy(at(B2 + 4096, 512), B(("Zp", o))).then_inc(*K.drained(("Zp", o)))

                def drain_oT(grp, gi, t):
                    job = ("oT", grp, t)
                    act.wait_ge(*K.full(job))
                    nc.scalar.copy(oT[:, 2 * gi:2 * gi + 2, t * P:(t + 1) * P],
                                   B(job, GW).rearrange("p (a n) -> p a n", a=2)).then_inc(*K.drained(job))

                for t in range(TT):
                    drain_oT("hy", 3, t)
                stage_end(act)

                def attention(grp, gi):
                    two = NMAPS[grp] == 2
                    scale = DK[grp] ** -0.5

                    def turned(i):
                        t, _ = UNITS[i]
                        if t == NT:
                            return
                        job = ("T", grp, i, 0) if two else ("T", grp, i)
                        if i >= 2:
                            act.wait_ge(*K.full(("O", grp, i - 2)))
                        act.wait_ge(*K.full(job))
                        nc.scalar.copy(at(PT + (i % 2) * TOK, 512), B(job)).then_inc(*K.drained(job))

                    def exps(i):
                        t, _ = UNITS[i]
                        for s in range(NMAPS[grp]):
                            job = ("S", grp, i, s)
                            act.wait_ge(*S.at("neg_max", (grp, i, s)))
                            slot = 2 if s == 1 else i % 2
                            if s == 1 and i >= 1:
                                act.wait_ge(*S.at("combined", i - 1))
                            elif i >= 2:
                                act.wait_ge(*K.full(("T", grp, i - 2, (n_keys(UNITS[i - 2][0]) - 1) // 4)
                                                    if two else ("T", grp, i - 2)))
                            nk = n_keys(t) * P
                            col = 16 * (i % 4) + 8 * s
                            g = s if two else i % 2
                            nc.scalar.activation(at(PB + slot * TOK, nk), score_view(g, nk), ACT.Exp,
                                                 bias=st[:, col + 1:col + 2], scale=scale,
                                                 accum_out=st[:, col + 2:col + 3]).then_inc(*K.drained(job))

                    lag = 1 if two else 2
                    for i in range(NU + lag + 1):
                        if 1 <= i <= NU:
                            turned(i - 1)
                        if i < NU:
                            exps(i)
                        n = i - lag - 1
                        if n >= 0 and n % NH == NH - 1:
                            drain_oT(grp, gi, UNITS[n][0])

                for i in range(TT + 3):
                    if i < TT:
                        job, z = ("proj", "mla", i), ZB + (i % 2) * WC
                        act.wait_ge(*K.full(job))
                        if i >= 2:
                            act.wait_ge(*K.full(("cT", i - 2)))
                            act.wait_ge(*S.at("k_rope_spread", i - 2))
                        nc.scalar.copy(at(z, 416), B(job, 416)).then_inc(*K.drained(job))
                        act.wait_ge(*K.emptied(job))
                        if i >= 1:
                            act.wait_ge(*S.at("latent_squares", i - 1))
                        nc.scalar.activation(at(PT, GW), at(z, GW), ACT.Square, accum_out=st[:, 4 * (i % 2):4 * (i % 2) + 1])
                        nc.scalar.activation(at(PT + GW, P), at(z + GW, P), ACT.Square,
                                             accum_out=st[:, 4 * (i % 2) + 1:4 * (i % 2) + 2]).then_inc(*S.up("latent_squares", i))
                    if 2 <= i <= TT + 1:
                        job, t = ("qT", i - 2), i - 2
                        if t < TT:
                            act.wait_ge(*K.full(job))
                            nc.scalar.copy(at(QT, NH, TOK, parts=96)[:, :, t * P:(t + 1) * P],
                                           B(job, parts=96).rearrange("p (h n) -> p h n", h=NH)).then_inc(*K.drained(job))
                    if 1 <= i <= TT + 1:
                        t = i - 1
                        if t < TT:
                            job = ("q", t)
                            act.wait_ge(*K.full(job))
                            if t >= 1:
                                act.wait_ge(*K.full(("qT", t - 1)))
                            nc.scalar.copy(at(QS, 384), B(job, 384)).then_inc(*K.drained(job))
                        job = ("kv", t)
                        act.wait_ge(*K.full(job))
                        if t >= 1:
                            act.wait_ge(*K.full(("kT", t - 1)))
                        kt = CACHE if t == TT else key_tile(t)
                        kv = B(job).rearrange("p (h n) -> p h n", h=NH)
                        nc.scalar.copy(at(VV + kt * GW, NH, 64), kv[:, :, 64:128])
                        nc.scalar.copy(at(QS + 384, NH, 96)[:, :, 0:64], kv[:, :, 0:64]).then_inc(*K.drained(job))
                for t in range(TT):
                    half_tanh("mla", t)
                act.wait_ge(*S.at("state_stored", "mla"))
                attention("mla", 0)
                stage_end(act)

                for gi, grp in ((1, "gqa"), (2, "diff")):
                    nk = 1 if grp == "gqa" else 2

                    def heads_turned(t):
                        job = ("hT", grp, t)
                        act.wait_ge(*K.full(job))
                        if t < TT:
                            nc.scalar.copy(at(QT, 4, TOK)[:, 0:2, t * P:(t + 1) * P],
                                           B(job, GW).rearrange("p (a n) -> p a n", a=2))
                        kt = CACHE if t == TT else key_tile(t)
                        nc.scalar.copy(at(KT, 4, NKEY * P)[:, 0:nk, kt * P:(kt + 1) * P],
                                       B(job)[:, GW:GW + nk * P].rearrange("p (a n) -> p a n", a=nk)
                                       ).then_inc(*K.drained(job))

                    act.wait_ge(*S.at(f"{grp}_params"))
                    for i in range(TT + 1):
                        if i < TT:
                            job, z = ("proj", grp, i), ZB + (i % 2) * WC
                            act.wait_ge(*K.full(job))
                            if i >= 2:
                                act.wait_ge(*K.full(("hT", grp, i - 2)))
                            ps = B(job)
                            if grp == "gqa":
                                nc.scalar.copy(at(z, 2, 2, 64), ps[:, 0:256].rearrange("p (g r n) -> p r g n", g=2, r=2))
                                nc.scalar.copy(at(z + 256, P), ps[:, 256:384])
                                nc.scalar.copy(at(VV + key_tile(i) * GW, P), ps[:, 384:512]).then_inc(*K.drained(job))
                            else:
                                nc.scalar.copy(at(z, 512), ps).then_inc(*K.drained(job))
                        if i >= 1:
                            heads_turned(i - 1)
                    heads_turned(TT)
                    for t in range(TT):
                        if grp == "diff":
                            act.wait_ge(*K.full(("gate", grp, t)))
                            nc.scalar.copy(at(VV + key_tile(t) * GW, GW), B(("gate", grp, t))[:, 0:GW])
                            half_tanh(grp, t, GW)
                        else:
                            half_tanh(grp, t)
                    if grp == "diff":
                        act.wait_ge(*S.at("lambda_sums"))
                        nc.scalar.activation(lamv[:, 2:4], lamv[:, 0:2], ACT.Exp).then_inc(*S.up("lambda_exps"))
                    act.wait_ge(*S.at("state_stored", grp))
                    attention(grp, gi)
                    stage_end(act)

                for t in range(TT):
                    for half in range(2):
                        job = ("y", t, half)
                        act.wait_ge(*K.full(job))
                        if t + half >= 1:
                            act.wait_ge(*S.at("out_squares", (t, 0) if half else (t - 1, 1)))
                        if t >= 2:
                            act.wait_ge(*K.emptied(("y", t - 2, 1)))
                        nc.scalar.activation(at(YN + 2 * D, 512), B(job), ACT.Square,
                                             accum_out=st[:, 8 * (t % 2) + half:8 * (t % 2) + half + 1]
                                             ).then_inc(*S.up("out_squares", (t, half)))
                stage_end(act)
                layer_end(act)

        @block.vector
        def _(v):
            def link(ins, name="vector_step", key=None):
                ins.then_inc(*S.up(name, key))
                v.wait_ge(*S.now(name))

            def tt(out, a, b, op):
                return nc.vector.tensor_tensor(out, a, b, op)

            def rstd(key, *parts):
                for x, n in parts:
                    last = nc.vector.tensor_scalar(x, x, 1.0 / n, EPS, ALU.mult, ALU.add)
                last.then_inc(*S.up("variance", key))
                v.wait_ge(*S.at("inverse_root", key))

            v.wait_ge(S.raw("silu_ready"), 1)
            nc.vector.scalar_tensor_tensor(csil[:, :, :], csil[:, :, :], 1.0, craw[:, :, :], ALU.add, ALU.mult
                                           ).then_inc(S.raw("silu_ready"), 1)
            v.wait_ge(S.raw("silu_ready"), 2)
            nc.vector.tensor_scalar(csil[:, :, :], csil[:, :, :], 0.5, None, ALU.mult).then_inc(S.raw("silu_ready"), 1)
            with v.Fori(0, DEPTH) as l:
                v.wait_ge(*S.at("ada_params"))
                mod = at(A_MOD, 3072, parts=2)
                for j in range(6):
                    v.wait_ge(*K.full(("ada", j)))
                    tt(mod[:, j * 512:(j + 1) * 512], B(("ada", j), parts=2),
                       at(A_ADAB + j * 512, 512, parts=2), ALU.add).then_inc(*K.drained(("ada", j)))
                v.wait_ge(*K.full(("modT",)))
                mt = B(("modT",), 4 * KD).rearrange("p (k s) -> p k s", s=2)
                nc.vector.tensor_copy(mcol[:, 0:KD, :], mt[:, 0:KD, :])
                nc.vector.scalar_tensor_tensor(mcol[:, KD:2 * KD, :], mt[:, KD:2 * KD, :], 1.0,
                                               gpre[:, :].unsqueeze(2).to_broadcast([P, KD, 2]), ALU.add, ALU.mult
                                               ).then_inc(*K.drained(("modT",)))
                for s in range(2):
                    for half in range(2):
                        job = ("gate_row", s, half)
                        v.wait_ge(*K.full(job))
                        tt(at(SGH + s * D + half * 512, 512), B(job), at(A_NPOST + half * 512, 512), ALU.mult
                           ).then_inc(*K.drained(job))
                stage_end(v)

                v.wait_ge(*S.at("filter_params"))
                x, kk = at(F_ARG, TOK, parts=64), at(F_K, TOK, parts=64)
                for n in (1, 2):
                    for i, (c, w) in enumerate(PARTS):
                        job = (f"f{n}", i)
                        v.wait_ge(*K.full(job))
                        if n == 2 and i == 0:
                            v.wait_ge(*K.full(("f2", 2)))
                        nc.vector.tensor_scalar(at(F_ARG + c, w, parts=64), B(job, w, 64), fwp[:, n - 1:n],
                                                fwp[:, n + 1:n + 2], ALU.add, ALU.mult).then_inc(*K.drained(job))
                        v.wait_ge(*K.emptied(job))
                    link(nc.vector.tensor_scalar(kk, x, 1.0 / TWO_PI, MAGIC, ALU.mult, ALU.add))
                    link(nc.vector.tensor_scalar(kk, kk, MAGIC, None, ALU.subtract))
                    for part in (PI_A, PI_B, PI_C):
                        link(nc.vector.scalar_tensor_tensor(x, kk, -part, x, ALU.mult, ALU.add))
                    nc.vector.tensor_scalar(x, x, -PI_SAFE, PI_SAFE, ALU.max, ALU.min).then_inc(*S.up("angle", n))

                def butterfly(key, src, mid, dst, sign):
                    E, M, X = at(src, 4, D), at(mid, 4, D), at(dst, 4, D)
                    link(tt(M[:, 0:2, :], E[:, 0:2, :], E[:, 2:4, :], ALU.add), "butterfly_sums", key)
                    if src == dst:
                        v.wait_ge(*S.at("butterfly_diffs", key))
                    tt(X[:, 0, :], M[:, 0, :], M[:, 1, :], ALU.add)
                    link(tt(X[:, 2, :], M[:, 0, :], M[:, 1, :], ALU.subtract), "butterfly_vector", key)

                eo = at(EO, TT, 3, GW)
                for o in (1, 0):
                    for t in range(TT):
                        job = ("f3", o, t)
                        v.wait_ge(*K.full(job))
                        v.wait_ge(*S.at("decay", t))
                        if o == 0 and t == 0:
                            v.wait_ge(*K.full(("FEp", 1)))
                        tt(eo[:, t, 0:2, :], B(job).rearrange("p (a n) -> p a n", a=2),
                           at(A_DEC + t * GW, GW).unsqueeze(1).to_broadcast([P, 2, GW]), ALU.mult
                           ).then_inc(*K.drained(job))
                        if t in (0, NT):
                            v.wait_ge(*K.emptied(job))
                            nc.vector.memset(eo[0:1, t, 1, :], 0.0).then_inc(*S.up("lag0_cleared", (o, t)))
                    for a0 in range(4):
                        for p in range(2):
                            v.wait_ge(*K.emptied(("FE", o, a0, p)))
                    E = at(B2, 4, 2, 2, GW)
                    bias = at(A_HBIAS + o * GW, GW)
                    for p in range(2):
                        link(nc.vector.scalar_tensor_tensor(E[:, 0, p, 0, :], bias, 1.0 / N_SAMPLE, E[:, 0, p, 0, :],
                                                            ALU.mult, ALU.add), "bias_added", (o, p))
                    if o == 0:
                        v.wait_ge(*S.at("spectrum1_kept"))
                    butterfly(("F", o), B2, B3, HS, -1)
                    v.wait_ge(*K.emptied(("FEp", o)))
                    nc.vector.scalar_tensor_tensor(at(HS + 4096, GW), bias, 1.0 / N_PROMPT, at(B2 + 4096, GW),
                                                   ALU.mult, ALU.add)
                    nc.vector.tensor_copy(at(HS + 4096 + GW, GW), at(B2 + 4096 + GW, GW)
                                          ).then_inc(*S.up(f"spectrum{o}_made"))
                stage_end(v)

                for t in range(TT + 1):
                    if t < TT:
                        v.wait_ge(*S.at("x_squares", t))
                        rstd(("x", t), (st[:, t:t + 1], D))
                        nc.vector.tensor_scalar(at(XN + (t % 2) * D, D), at(XN + (t % 2) * D, D), st[:, t:t + 1],
                                                None, ALU.mult).then_inc(*S.up("x_normed", t))
                    if t >= 1:
                        job, s = ("xT", t - 1, 1), int(t - 1 == NT)
                        v.wait_ge(*K.full(job))
                        for k in range(4):
                            last = nc.vector.tensor_scalar(hT[:, 4 + k, (t - 1) * P:t * P], B(job)[:, k * P:(k + 1) * P],
                                                           mcol[:, KD + 4 + k, s:s + 1], mcol[:, 4 + k, s:s + 1],
                                                           ALU.mult, ALU.add)
                        last.then_inc(*K.drained(job))
                stage_end(v)

                xv = at(XV, TT, 768)

                def drain_uT(f):
                    for g in (1, 2):
                        job, n = ("uT", f, g), (4 if g == 1 else 1)
                        v.wait_ge(*K.full(job))
                        nc.vector.tensor_copy(xv[:, 4 * g:4 * g + n, f * P:(f + 1) * P],
                                              B(job, n * P).rearrange("p (a n) -> p a n", a=n)).then_inc(*K.drained(job))

                for f in range(6):
                    u, c = U0 + (f % 2) * UW, CU + (f % 2) * TOK
                    v.wait_ge(*S.at("middle_tap", f))
                    v.wait_ge(*S.at("edges", f))
                    for tap, shift in ((0, 0), (2, 2)):
                        ins = [nc.vector.scalar_tensor_tensor(at(c, D), at(u + shift * P, D), hcw[:, f, tap:tap + 1],
                                                              at(c, D), ALU.mult, ALU.add),
                               nc.vector.scalar_tensor_tensor(at(c + D, P), at(u + 10 * P + shift, P),
                                                              hcw[:, f, tap:tap + 1], at(c + D, P), ALU.mult, ALU.add)]
                        if tap == 0:
                            link(ins[1])
                        else:
                            ins[1].then_inc(*S.up("taps", f))
                    if f >= 1:
                        drain_uT(f - 1)

                def finish_gate(grp, t, dst, c0=0):
                    job = ("gate", grp, t)
                    v.wait_ge(*S.at("half_tanh", (grp, t)))
                    th = (CU + 2 * TOK if grp == "hy" else OB) + (t % 2) * GW
                    nc.vector.scalar_tensor_tensor(at(dst + t * GW, GW), at(th, GW), 1.0, B(job)[:, c0:c0 + GW],
                                                   ALU.add, ALU.mult).then_inc(*K.drained(job))

                v.wait_ge(*S.at("gate_rows_kept"))
                for t in range(TT):
                    finish_gate("hy", t, SGH)
                    if t == 1:
                        drain_uT(5)
                stage_end(v)

                zv = at(XV, TT, 3, GW)
                for o in range(2):
                    if o == 1:
                        v.wait_ge(*K.full(("Y", 0, 3)))
                    for a0 in range(4):
                        job = ("Z", o, a0, 1)
                        v.wait_ge(*K.full(job))
                        nc.vector.tensor_copy(at(B2 + (a0 * 2 + 1) * 512, 512), B(job)).then_inc(*K.drained(job))
                    for a0 in range(4):
                        for p in range(2):
                            v.wait_ge(*K.emptied(("Z", o, a0, p)))
                    butterfly(("X", o), B2, B3, B2, -1)
                    if o == 1:
                        v.wait_ge(*S.at("spectrum1_back"))
                    v.wait_ge(*S.at("butterfly_pool", ("X", o)))
                    H, X, T1 = (at(off, 8, 2, GW) for off in (HS, B2, B3))
                    h4 = slice(0, 4)
                    link(tt(T1[:, h4, :, :], H[:, h4, :, :], X[:, h4, :, :], ALU.mult))
                    link(tt(T1[:, h4, 0, :], T1[:, h4, 0, :], T1[:, h4, 1, :], ALU.subtract))
                    tt(T1[:, h4, 1, :], H[:, h4, 0, :], X[:, h4, 1, :], ALU.mult)
                    link(tt(X[:, h4, 0, :], H[:, h4, 1, :], X[:, h4, 0, :], ALU.mult))
                    link(tt(T1[:, h4, 1, :], T1[:, h4, 1, :], X[:, h4, 0, :], ALU.add), "product_rows_vector", o)
                    v.wait_ge(*K.emptied(("Zp", o)))
                    Hp, Xp, Tp = (at(off + 4096, 2, GW) for off in (HS, B2, B3))
                    link(tt(Tp[:, :, :], Hp[:, :, :], Xp[:, :, :], ALU.mult))
                    link(tt(Tp[:, 0, :], Tp[:, 0, :], Tp[:, 1, :], ALU.subtract))
                    tt(Tp[:, 1, :], Hp[:, 0, :], Xp[:, 1, :], ALU.mult)
                    link(tt(Xp[:, 0, :], Hp[:, 1, :], Xp[:, 0, :], ALU.mult), "product_vector", o)
                    tt(Tp[:, 1, :], Tp[:, 1, :], Xp[:, 0, :], ALU.add).then_inc(*S.up("product_prompt", o))
                    v.wait_ge(*S.at("product_pool", o))
                    butterfly(("G", o), B3, B2, B3, 1)
                    for i in range(4):
                        job = ("Y", o, i)
                        v.wait_ge(*K.full(job))
                        tt(zv[:, 2 * i:2 * i + 2, 2, :], B(job).rearrange("p (a n) -> p a n", a=2),
                           zv[:, 2 * i:2 * i + 2, o, :], ALU.mult).then_inc(*K.drained(job))
                    v.wait_ge(*K.full(("Yp", o)))
                    tt(zv[:, NT, 2, :], B(("Yp", o), GW), zv[:, NT, o, :], ALU.mult).then_inc(*K.drained(("Yp", o)))
                for t in range(TT):
                    v.wait_ge(*K.emptied(("Y", 1, t // 2) if t < NT else ("Yp", 1)))
                    nc.vector.scalar_tensor_tensor(zv[:, t, 2, :], zv[:, t, 2, :], 0.5, at(SGH + t * GW, GW),
                                                   ALU.mult, ALU.mult).then_inc(*S.up("gated", ("hy", t)))
                stage_end(v)

                def rope(x, heads, n, t, key):
                    m = n // 4
                    tab = ROPE + t * 192 + (0 if n == 32 else 64)
                    cos, sin = at(tab, n), at(tab + n, n)
                    t1 = at(ROT, heads, n)
                    t2 = at(ROT + 512, heads, n)
                    tt(t1, x, cos.unsqueeze(1).to_broadcast([P, heads, n]), ALU.mult)
                    for s in range(2):
                        for j in range(2):
                            a, b = (2 * s + j) * m, (2 * s + 1 - j) * m
                            last = tt(t2[:, :, a:a + m], x[:, :, b:b + m],
                                      sin[:, a:a + m].unsqueeze(1).to_broadcast([P, heads, m]), ALU.mult)
                    link(last)
                    link(tt(x, t1, t2, ALU.add), *key)

                def attention(grp):
                    two = NMAPS[grp] == 2
                    scale = DK[grp] ** -0.5

                    def maxima(i):
                        t, _ = UNITS[i]
                        nk = n_keys(t) * P
                        for s in range(NMAPS[grp]):
                            col = 16 * (i % 4) + 8 * s
                            v.wait_ge(*K.full(("S", grp, i, s)))
                            if i >= 2:
                                v.wait_ge(*K.emptied(("S", grp, i - 2, s)))
                            link(nc.vector.tensor_reduce(st[:, col:col + 1], score_view(s if two else i % 2, nk),
                                                         AX.X, ALU.max))
                            nc.vector.tensor_scalar(st[:, col + 1:col + 2], st[:, col:col + 1], -scale, None, ALU.mult
                                                    ).then_inc(*S.up("neg_max", (grp, i, s)))

                    def turned(i):
                        t, _ = UNITS[i]
                        if i >= 2:
                            v.wait_ge(*K.full(("O", grp, i - 2)))
                        pt = PT + (i % 2) * TOK
                        if not two:
                            job = ("T", grp, i)
                            v.wait_ge(*K.full(job))
                            if t == NT:
                                nc.vector.tensor_copy(at(pt, P), score_view(i % 2, P)).then_inc(*K.drained(job))
                            else:
                                nc.vector.tensor_copy(at(pt + 512, TOK - 512), score_view(i % 2, TOK)[:, 512:TOK]
                                                      ).then_inc(*K.drained(job))
                            return
                        for b in ((0,) if t == NT else (1, 2)):
                            job, n = ("T", grp, i, b), (512 if b == 1 else P)
                            v.wait_ge(*K.full(job))
                            nc.vector.tensor_copy(at(pt + b * 512, n), B(job, n)).then_inc(*K.drained(job))

                    def weigh(i):
                        c0, c1 = 16 * (i % 4), 16 * (i % 4) + 8
                        for s in range(2):
                            v.wait_ge(*K.emptied(("S", grp, i, s)))
                        if i >= 2:
                            v.wait_ge(*S.at("combined", i - 2))
                        link(nc.vector.reciprocal(st[:, c1 + 3:c1 + 4], st[:, c1 + 2:c1 + 3]))
                        nc.vector.scalar_tensor_tensor(st[:, c1 + 4:c1 + 5], st[:, c1 + 3:c1 + 4], st[:, c0 + 2:c0 + 3],
                                                       lamv[:, 6:7], ALU.mult, ALU.mult).then_inc(*S.up("weight", i))

                    def finish(i):
                        t, h = UNITS[i]
                        c0 = 16 * (i % 4)
                        rc = st[:, c0 + 5:c0 + 6]
                        v.wait_ge(*K.emptied(("S", grp, i, 0)))
                        link(nc.vector.reciprocal(rc, st[:, c0 + 2:c0 + 3]))
                        v.wait_ge(*K.full(("O", grp, i)))
                        if h == 0 and t >= 2:
                            v.wait_ge(*K.full(("oT", grp, t - 2)))
                        o = OB + (t % 2) * GW
                        nc.vector.tensor_scalar(at(o + h * 64, 64), B(("O", grp, i), 64), rc, None, ALU.mult
                                                ).then_inc(*K.drained(("O", grp, i)))
                        if h < NH - 1:
                            return
                        v.wait_ge(*K.emptied(("O", grp, i)))
                        if two:
                            r4 = st[:, 64:68]
                            sq = at(QS, GW)
                            link(tt(sq, at(o, GW), at(o, GW), ALU.mult))
                            link(nc.vector.tensor_reduce(r4, at(QS, NH, 64), AX.X, ALU.add))
                            rstd(("diff_out", t), (r4, 64))
                            link(tt(at(o, NH, 64), at(o, NH, 64), r4.unsqueeze(2).to_broadcast([P, NH, 64]), ALU.mult))
                            link(tt(at(o, NH, 64), at(o, NH, 64),
                                    at(WQB, 64).unsqueeze(1).to_broadcast([P, NH, 64]), ALU.mult))
                        nc.vector.scalar_tensor_tensor(at(o, GW), at(o, GW), 0.5, at(SG + t * GW, GW),
                                                       ALU.mult, ALU.mult).then_inc(*S.up("gated", (grp, t)))

                    lag = 1 if two else 2
                    for i in range(NU + lag):
                        if i < NU:
                            maxima(i)
                        if 1 <= i <= NU:
                            turned(i - 1)
                        if lag <= i:
                            finish(i - lag)
                        if two and i < NU:
                            weigh(i)

                v.wait_ge(*S.at("mla_params"))
                v.wait_ge(*S.at("mla_gains"))

                def latent_turned(t):
                    job = ("cT", t)
                    v.wait_ge(*K.full(job))
                    if t >= 1:
                        v.wait_ge(*K.full(("kv", t - 1)))
                    if t == TT:
                        nc.vector.tensor_copy(at(CT + 2 * P, P), B(job)[:, 2 * P:3 * P]).then_inc(*K.drained(job))
                        return
                    for i in range(3):
                        last = nc.vector.tensor_scalar(at(CT + i * P, P), B(job)[:, i * P:(i + 1) * P], mg[:, i:i + 1],
                                                       None, ALU.mult)
                    last.then_inc(*K.drained(job))

                for i in range(TT + 3):
                    if i < TT:
                        c, z = 4 * (i % 2), ZB + (i % 2) * WC
                        v.wait_ge(*S.at("latent_squares", i))
                        rstd(("latent", i), (st[:, c:c + 1], 256), (st[:, c + 1:c + 2], P))
                        link(nc.vector.tensor_scalar(at(z, GW), at(z, GW), st[:, c:c + 1], None, ALU.mult))
                        link(nc.vector.tensor_scalar(at(z + GW, P), at(z + GW, P), st[:, c + 1:c + 2], None, ALU.mult),
                             "latent", i)
                        if i < NT:
                            rope(at(z + 384, 1, 32), 1, 32, i, ("k_roped", i))
                        else:
                            tt(at(CKVOUT, P), at(z + GW, P), at(KVGAIN, P), ALU.mult).then_inc(*S.up("state_ready", "mla"))
                    if i == TT:
                        nc.vector.memset(st[:, 72:73], 0.0).then_inc(*S.up("latent", TT))
                    if 1 <= i <= TT + 1:
                        latent_turned(i - 1)
                    if 2 <= i <= TT + 2:
                        t = i - 2
                        job = ("kT", t)
                        kt = CACHE if t == TT else key_tile(t)
                        v.wait_ge(*K.full(job))
                        nc.vector.tensor_copy(at(KT, NH, NKEY * P, parts=96)[:, :, kt * P:(kt + 1) * P],
                                              B(job, parts=96).rearrange("p (h n) -> p h n", h=NH)).then_inc(*K.drained(job))
                    if 1 <= i <= TT:
                        t = i - 1
                        v.wait_ge(*K.emptied(("q", t)))
                        if t < NT:
                            rope(at(QS, NH, 96)[:, :, 64:96], NH, 32, t, ("q_roped", t))
                        else:
                            nc.vector.memset(st[:, 72:73], 0.0).then_inc(*S.up("q_roped", t))
                for t in range(TT):
                    finish_gate("mla", t, SG)
                attention("mla")
                stage_end(v)

                for grp, nh, n in (("gqa", 6, 64), ("diff", 16, 32)):
                    v.wait_ge(*S.at(f"{grp}_params"))
                    if grp == "diff":
                        q = at(WQB + 64, 4, 32)
                        for i in range(2):
                            link(tt(at(SQ + 32 * i, 32), q[:, 2 * i, :], q[:, 2 * i + 1, :], ALU.mult))
                        nc.vector.tensor_reduce(lamv[:, 0:2], at(SQ, 2, 32), AX.X, ALU.add).then_inc(*S.up("lambda_sums"))
                        link(nc.vector.tensor_scalar(at(WQB, 64), at(WQB, 64), lamv[:, 5:6], None, ALU.mult))
                    for i in range(TT + 1):
                        if i < TT:
                            z = ZB + (i % 2) * WC
                            v.wait_ge(*K.emptied(("proj", grp, i)))
                            if grp == "gqa":
                                r6 = st[:, 8 * (i % 2):8 * (i % 2) + 6]
                                link(tt(at(SQ, 384), at(z, 384), at(z, 384), ALU.mult))
                                link(nc.vector.tensor_reduce(r6, at(SQ, 6, 64), AX.X, ALU.add))
                                rstd(("heads", i), (r6, 64))
                                link(tt(at(z, 6, 64), at(z, 6, 64), r6.unsqueeze(2).to_broadcast([P, 6, 64]), ALU.mult))
                                link(tt(at(z, 384), at(z, 384), at(WQB, 384), ALU.mult),
                                     *(("state_ready", "gqa") if i == NT else ("vector_step", None)))
                            if i < NT:
                                rope(at(z, nh, n), nh, n, i, ("heads_ready", (grp, i)))
                            else:
                                nc.vector.memset(st[:, 72:73], 0.0).then_inc(*S.up("heads_ready", (grp, i)))
                    for t in range(TT):
                        finish_gate(grp, t, SG, 0 if grp == "gqa" else GW)
                    if grp == "diff":
                        v.wait_ge(*S.at("lambda_exps"))
                        link(tt(lamv[:, 6:7], lamv[:, 3:4], lamv[:, 2:3], ALU.subtract))
                        link(tt(lamv[:, 6:7], lamv[:, 6:7], lamv[:, 4:5], ALU.subtract))
                    attention(grp)
                    stage_end(v)

                v.wait_ge(*S.at("gate_rows_back"))
                for t in range(TT):
                    c = 8 * (t % 2)
                    s = int(t == NT)
                    v.wait_ge(*S.at("out_squares", (t, 1)))
                    link(tt(st[:, c + 2:c + 3], st[:, c:c + 1], st[:, c + 1:c + 2], ALU.add))
                    rstd(("out", t), (st[:, c + 2:c + 3], D))
                    if t >= 2:
                        v.wait_ge(*S.at("x_updated", t - 2))
                    for half in range(2):
                        job = ("y", t, half)
                        nc.vector.scalar_tensor_tensor(at(YN + (t % 2) * D + half * 512, 512), B(job), st[:, c + 2:c + 3],
                                                       at(GR + s * D + half * 512, 512), ALU.mult, ALU.mult
                                                       ).then_inc(*K.drained(job))
                stage_end(v)
                layer_end(v)

        @block.gpsimd
        def _(pool):
            def link(ins, name="pool_step", key=None):
                ins.then_inc(*S.up(name, key))
                pool.wait_ge(*S.now(name))

            def tt(out, a, b, op):
                return nc.gpsimd.tensor_tensor(out, a, b, op)

            def inverse_root(key, x):
                pool.wait_ge(*S.at("variance", key))
                tt(x, x, mhalf[:, 0:x.shape[1]], ALU.pow).then_inc(*S.up("inverse_root", key))

            nc.gpsimd.memset(mhalf[:, :], -0.5).then_inc(S.raw("exponent_set"), 1)
            pool.wait_ge(S.raw("exponent_set"), 1)
            with pool.Fori(0, DEPTH) as l:
                stage_end(pool)

                def butterfly(key, src, mid, dst, sign):
                    E, M, X = at(src, 4, 2, 2, GW), at(mid, 4, 2, 2, GW), at(dst, 4, 2, 2, GW)
                    link(tt(at(mid + 2 * D, 2 * D), at(src, 2 * D), at(src + 2 * D, 2 * D), ALU.subtract),
                         "butterfly_diffs", key)
                    if src == dst:
                        pool.wait_ge(*S.at("butterfly_sums", key))
                    lo, hi = (1, 3) if sign < 0 else (3, 1)
                    tt(X[:, lo, :, 0, :], M[:, 2, :, 0, :], M[:, 3, :, 1, :], ALU.add)
                    tt(X[:, lo, :, 1, :], M[:, 2, :, 1, :], M[:, 3, :, 0, :], ALU.subtract)
                    tt(X[:, hi, :, 0, :], M[:, 2, :, 0, :], M[:, 3, :, 1, :], ALU.subtract)
                    link(tt(X[:, hi, :, 1, :], M[:, 2, :, 1, :], M[:, 3, :, 0, :], ALU.add), "butterfly_pool", key)

                eo = at(EO, TT, 3, GW)
                for o in (1, 0):
                    for t in range(TT):
                        pool.wait_ge(*K.emptied(("f3", o, t)))
                        if t in (0, NT):
                            pool.wait_ge(*S.at("lag0_cleared", (o, t)))
                        last = nc.gpsimd.tensor_scalar(eo[:, t, 2, :], eo[:, t, 1, :], -1.0, None, ALU.mult)
                    last.then_inc(*S.up("filter_negated", o))
                    for a0 in range(4):
                        for p in range(2):
                            pool.wait_ge(*K.emptied(("FE", o, a0, p)))
                    pool.wait_ge(*S.at("bias_added", (o, 1)))
                    if o == 0:
                        pool.wait_ge(*S.at("spectrum1_kept"))
                    butterfly(("F", o), B2, B3, HS, -1)
                stage_end(pool)
                for t in range(TT):
                    inverse_root(("x", t), st[:, t:t + 1])
                stage_end(pool)

                for half in range(2):
                    u = U0 + half * UW
                    nc.gpsimd.memset(at(u, 1), 0.0)
                    nc.gpsimd.memset(at(u + 9 * P + P - 1, 1), 0.0)
                    nc.gpsimd.memset(at(u + 10 * P, 1), 0.0)
                    link(nc.gpsimd.memset(at(u + 10 * P + 129, 1), 0.0))
                for f in range(6):
                    u = U0 + (f % 2) * UW
                    for i in range(3):
                        pool.wait_ge(*K.emptied(("u", f, i)))
                    nc.gpsimd.tensor_copy(at(u + 1, P - 1), at(u + 8 * P, P - 1))
                    nc.gpsimd.tensor_copy(at(u + 9 * P, P - 1), at(u + P + 1, P - 1)).then_inc(*S.up("edges", f))
                stage_end(pool)

                for o in range(2):
                    for a0 in range(4):
                        for p in range(2):
                            pool.wait_ge(*K.emptied(("Z", o, a0, p)))
                    butterfly(("X", o), B2, B3, B2, -1)
                    if o == 1:
                        pool.wait_ge(*S.at("spectrum1_back"))
                    pool.wait_ge(*S.at("butterfly_vector", ("X", o)))
                    H, X, T1 = (at(off, 8, 2, GW) for off in (HS, B2, B3))
                    h4 = slice(4, 8)
                    link(tt(T1[:, h4, :, :], H[:, h4, :, :], X[:, h4, :, :], ALU.mult))
                    link(tt(T1[:, h4, 0, :], T1[:, h4, 0, :], T1[:, h4, 1, :], ALU.subtract))
                    tt(T1[:, h4, 1, :], H[:, h4, 0, :], X[:, h4, 1, :], ALU.mult)
                    link(tt(X[:, h4, 0, :], H[:, h4, 1, :], X[:, h4, 0, :], ALU.mult))
                    link(tt(T1[:, h4, 1, :], T1[:, h4, 1, :], X[:, h4, 0, :], ALU.add), "product_pool", o)
                    pool.wait_ge(*S.at("product_rows_vector", o))
                    butterfly(("G", o), B3, B2, B3, 1)
                stage_end(pool)

                pool.wait_ge(*S.at("mla_params"))
                for t in range(TT + 1):
                    if t < TT:
                        inverse_root(("latent", t), st[:, 4 * (t % 2):4 * (t % 2) + 2])
                    if t < NT:
                        pool.wait_ge(*S.at("k_roped", t))
                    elif t == NT:
                        pool.wait_ge(*K.emptied(("proj", "mla", t)))
                    if t >= 1:
                        pool.wait_ge(*K.full(("kT", t - 1)))
                    src = at(CROPE, 32) if t == TT else at(ZB + (t % 2) * WC + 384, 32)
                    nc.gpsimd.tensor_copy(at(QS + 384, NH, 96)[:, :, 64:96],
                                          src.unsqueeze(1).to_broadcast([P, NH, 32])).then_inc(*S.up("k_rope_spread", t))
                stage_end(pool)
                for t in range(TT):
                    inverse_root(("heads", t), st[:, 8 * (t % 2):8 * (t % 2) + 6])
                stage_end(pool)

                for i, (t, h) in enumerate(UNITS):
                    if h == 0 and i:
                        inverse_root(("diff_out", UNITS[i - 1][0]), st[:, 64:68])
                    pool.wait_ge(*S.at("weight", i))
                    n = n_keys(t) * P
                    c1 = 16 * (i % 4) + 8
                    p0 = at(PB + (i % 2) * TOK, n)
                    link(nc.gpsimd.tensor_scalar(at(PB + 2 * TOK, n), at(PB + 2 * TOK, n), st[:, c1 + 4:c1 + 5], None,
                                                 ALU.mult))
                    tt(p0, at(PB + 2 * TOK, n), p0, ALU.add).then_inc(*S.up("combined", i))
                inverse_root(("diff_out", NT), st[:, 64:68])
                stage_end(pool)

                for t in range(TT):
                    inverse_root(("out", t), st[:, 8 * (t % 2) + 2:8 * (t % 2) + 3])
                    pool.wait_ge(*K.emptied(("y", t, 0)))
                    pool.wait_ge(*K.emptied(("y", t, 1)))
                    pool.wait_ge(*S.at(f"xr{t % 3}_loaded", t))
                    x = at(XR + (t % 3) * D, D)
                    tt(x, x, at(YN + (t % 2) * D, D), ALU.add).then_inc(*S.up("x_updated", t))
                stage_end(pool)
                layer_end(pool)

        return S.count, S.mark, K.jobs


def tables():
    f = np.float32
    token = (NT * np.arange(P)[:, None] + np.arange(NT)[None, :])
    row, col = (token // 64).astype(f), (token % 64).astype(f)

    def axial(n):
        m = n // 2
        inv = (f(10000.0) ** (-np.arange(0, m, 2, dtype=f) / f(m))).astype(f)
        cos, sin = [], []
        for pos in (row, col):
            ang = (pos[..., None] * inv).astype(f)
            cos += [np.cos(ang), np.cos(ang)]
            sin += [-np.sin(ang), np.sin(ang)]
        return np.concatenate(cos, -1), np.concatenate(sin, -1)

    c32, s32 = axial(32)
    c64, s64 = axial(64)
    rope = np.concatenate([c32, s32, c64, s64], -1).astype(f)

    def feats(n):
        t = np.linspace(0.0, 1.0, n, dtype=f)[:, None]
        w = (f(2.0 * math.pi) * np.arange(n, dtype=f)[:, None] / f(n)).astype(f)
        fr = np.linspace(1e-4, 15, 16, dtype=f)[None, :]
        return np.concatenate([t, np.cos(fr * w), -np.sin(fr * w)], -1).astype(f), t[:, 0]

    fs, ts = feats(N_SAMPLE)
    fp, tp = feats(N_PROMPT)
    order = token.T.reshape(-1)
    ft = np.concatenate([fs[order], fp], 0).T
    negt = -np.concatenate([ts[token], tp[:, None]], 1)
    f2 = np.arange(P)
    tab = np.zeros((P, NT, 2, 2, P))
    for a in range(NT):
        for p in range(2):
            ang = math.pi * (2 * (f2[None, :] + 256 * p) + 1) * (8 * np.arange(P)[:, None] + a) / 2048.0
            tab[:, a, p, 0, :], tab[:, a, p, 1, :] = np.cos(ang), -np.sin(ang)
    inv = tab.transpose(4, 1, 2, 3, 0)
    sel = np.zeros((2, 2, P), f)
    sel[0, 0], sel[1, 1] = 1, 1
    lam = np.array([[0.8 - 0.6 * math.exp(-0.3 * i), 1.0 - (0.8 - 0.6 * math.exp(-0.3 * i))] for i in range(DEPTH)], f)
    return {"rope": rope, "feats": ft.astype(f), "negt": negt.astype(f), "sel": sel,
            "tab_f": tab.reshape(P, -1).astype(f), "tab_i": inv.reshape(P, -1).astype(f),
            "ident": np.eye(P, dtype=f), "lam_init": lam}


DIRECT = ["cache_mla_ckv", "cache_mla_krope", "cache_gqa_k", "cache_gqa_v", "cache_diff_k", "cache_diff_v",
          "c", "c_ctx", "norm_pre", "norm_post", "ada_w", "ada_b", "w_in", "w_out", "mla_q_norm", "mla_wq_b",
          "mla_kv_norm", "mla_wkv_b", "gqa_q_norm", "gqa_k_norm", "diff_lq1", "diff_lk1", "diff_lq2", "diff_lk2",
          "diff_subln", "hy_conv_w", "hy_conv_b", "hy_fw1", "hy_fb1", "hy_fw2", "hy_fb2", "hy_fw3", "hy_freq",
          "hy_decay"]
OUTS = {"xs": (DEPTH + 1, TOK, D), "new_mla_ckv": (1, DEPTH, P, 128), "new_mla_krope": (1, DEPTH, P, 32),
        "new_gqa_k": (1, DEPTH, P, 2, 64), "new_gqa_v": (1, DEPTH, P, 2, 64),
        "new_diff_k": (1, DEPTH, P, 4, 64), "new_diff_v": (1, DEPTH, P, 4, 64)}


def build(nc, arrays, known):
    ins = {n: nc.dram_tensor(f"in_{n}", list(a.shape), F32, kind="ExternalInput").ap() for n, a in arrays.items()}
    outs = {n: nc.dram_tensor(f"out_{n}", list(s), F32, kind="ExternalOutput").ap() for n, s in OUTS.items()}
    outs["spectrum_kept"] = nc.dram_tensor("spectrum_kept", [P, 4608], F32, kind="Internal").ap()
    outs["gates_kept"] = nc.dram_tensor("gates_kept", [P, 2 * D], F32, kind="Internal").ap()
    return program(nc, ins, outs, known)


def kernel(**inputs):
    import concourse.bacc as bacc
    from concourse.bass_utils import run_bass_kernel_spmd

    arrays = {n: np.ascontiguousarray(inputs[n]) for n in DIRECT}
    arrays["x"] = np.concatenate([np.asarray(inputs["x_sample"])[0], np.asarray(inputs["x_prompt"])[0]], 0)
    arrays["hy_bias2"] = np.ascontiguousarray(inputs["hy_bias"]).reshape(DEPTH, 512)
    arrays.update(tables())
    known = None
    for _ in range(2):
        nc = bacc.Bacc("TRN2", target_bir_lowering=False, num_devices=1)
        known = build(nc, arrays, known)
    r = run_bass_kernel_spmd(nc, [{f"in_{n}": a for n, a in arrays.items()}], core_ids=[0]).results[0]
    x = r["out_xs"][DEPTH]
    return (x[NT * P:][None], x[:NT * P][None]) + tuple(r[f"out_{n}"] for n in list(OUTS)[1:])
```

```python
import math
from contextlib import ExitStack

import concourse.bass as bass
import numpy as np
from concourse import mybir

F32 = mybir.dt.float32
F32R = mybir.dt.float32r
ACT = mybir.ActivationFunctionType
ALU = mybir.AluOpType
AX = mybir.AxisListType

P = 128
D = 1024
KD = D // P
DEPTH = 2
NT = 8
TT = NT + 1
TOK = TT * P
CACHE, PROMPT = NT, NT + 1
NKEY = NT + 2
GW = 256
MLA_HEADS = 4
EPS = 1e-6
WC = 512
CHUNKS = {"hy0": (2464, 512), "hy1": (2976, 512), "mla": (0, 416), "mla_gate": (416, 256),
          "gqa": (672, 512), "gqa_gate": (1184, 256), "diff": (1440, 512), "diff_vg": (1952, 512)}
STREAM = [("ada", j) for j in range(6)] + [(c, 0) for c in CHUNKS] + [("out", 0), ("out", 1)]
SLOT = {c: n % 2 for n, c in enumerate(STREAM)}
LAST_JOB = {**{("ada", j): ("ada", j) for j in range(6)},
            ("hy0", 0): ("u", 3, 2), ("hy1", 0): ("gate", "hy", NT),
            ("mla", 0): ("proj", "mla", NT), ("mla_gate", 0): ("gate", "mla", NT),
            ("gqa", 0): ("proj", "gqa", NT), ("gqa_gate", 0): ("gate", "gqa", NT),
            ("diff", 0): ("proj", "diff1", NT), ("diff_vg", 0): ("gate", "diff", NT)}
PARTS = ((0, 512), (512, 512), (1024, 128))
TWO_PI = 2.0 * math.pi
PI_A = 6.28125
PI_B = math.floor((TWO_PI - PI_A) * 2 ** 23) / 2 ** 23
PI_C = TWO_PI - PI_A - PI_B
MAGIC = 12582912.0
PI_SAFE = 3.1415925
N_SAMPLE, N_PROMPT = NT * P, P

HT = 0
W0 = HT + KD * TOK
OT = W0 + 2 * KD * WC
FREE = OT + KD * TOK
A_MOD, A_ADAB, A_NPOST, A_FW3, A_FW = HT, HT + 3072, HT + 6144, HT + 7168, HT + 8192
A_HBIAS, A_DECAY = HT + 8320, HT + 8832
EO = OT
A_DEC = EO + TT * 3 * GW
TF = FREE
TI = TF + 4096
SGH = TI + 4096
HS = SGH + TT * GW
B2 = HS + 4608
B3 = B2 + 4608
GATE_T = B3 + 4608
HY_END = GATE_T + 2 * GW
XV = OT
F_FEAT, F_ARG, F_K = TI, TI + TOK, TI + 2 * TOK
U0 = B2
UW = 10 * P + 130
CU = U0 + 2 * UW
SG = FREE
ROPE = SG + TT * GW
QT = ROPE + NT * 192
KT = QT + 4 * TOK
VV = KT + 4 * NKEY * P
PB = VV + NKEY * GW
PT = PB + 3 * TOK
OB = PT + 2 * TOK
ZB = OB + 2 * GW
WQB = ZB + 2 * WC
WKVB = WQB + 768
CT = WKVB + 512
QS = CT + 384
ATT_END = QS + 768
ROT, SQ, AUX = PB, PB + 1024, PB + 2048
SPLIT = PT
KVGAIN, CKEY, CROPE, CKVOUT = AUX, AUX + 128, AUX + 384, AUX + 416
XN = B2
XR, GR, YN = FREE, FREE + 3 * D, FREE + 5 * D
NARENA = max(ATT_END, HY_END)
STAGES = ["filter", "norm", "hyena_in", "hyena", "mla", "gqa", "diff0", "diff1", "out"]
HEADS = {"mla": (0, 1, 2, 3), "gqa": (0, 1, 2, 3), "diff0": (0, 1), "diff1": (2, 3)}
NMAPS = {"mla": 1, "gqa": 1, "diff0": 2, "diff1": 2}
DK = {"mla": 96, "gqa": 64, "diff0": 32, "diff1": 32}
OUT_TILE = {"mla": 0, "gqa": 2, "diff0": 4, "diff1": 5, "hy": 6}
UNITS = {g: [(t, h) for t in range(TT) for h in HEADS[g]] for g in HEADS}
SPLIT_W = {"gqa": 896, "diff0": 768, "diff1": 768}
N_CONST = 5


def key_tile(t):
    return PROMPT if t == NT else t


def n_keys(t):
    return 1 if t == NT else NT + 1


class Signals:

    ONCE = ("constants", "x_copied", "silu_ready", "exponent_set", "layer_finished", "semaphores_cleared", "layer_entered")

    def __init__(self, nc, ctx, known):
        self.nc, self.ctx, self.known = nc, ctx, known
        self.sem, self.count, self.mark = {}, {}, {}
        for name in self.ONCE:
            self.raw(name)
        for name in (known[0] if known else ()):
            self.raw(name)

    def raw(self, name):
        if name not in self.sem:
            self.sem[name] = self.ctx.enter_context(self.nc.semaphore(name))
            self.count[name] = 0
        return self.sem[name]

    def counted_by_layer(self):
        numbers = [s.num for n, s in self.sem.items() if n not in self.ONCE]
        assert not self.known or sorted(numbers) == list(range(min(numbers), max(numbers) + 1))
        return range(min(numbers), max(numbers) + 1)

    def up(self, name, key=None, n=1):
        s = self.raw(name)
        self.count[name] += n
        self.mark[name, key] = self.count[name]
        return s, n

    def now(self, name):
        return self.raw(name), self.count[name]

    def at(self, name, key=None):
        return self.raw(name), (self.known[1][name, key] if self.known else 1)

    def all(self, name):
        return self.raw(name), (self.known[0][name] if self.known else 1)


class Banks:

    def __init__(self, signals, known):
        self.s, self.known = signals, known
        self.filled, self.drains, self.last, self.jobs = {}, {}, {}, {}
        self.turn = 0

    def next(self):
        self.turn += 1
        return [self.turn % 8]

    def claim(self, job, banks, drains=1):
        found = {self.last[b] for b in banks if b in self.last}
        b0 = banks[0]
        self.filled[b0] = self.filled.get(b0, 0) + 1
        self.drains[b0] = self.drains.get(b0, 0) + drains
        for b in banks:
            self.last[b] = (b0, self.drains[b0])
        assert job not in self.jobs, job
        self.jobs[job] = (b0, self.filled[b0], self.drains[b0])
        return [(self.s.raw(f"bank{b}_drained"), v) for b, v in sorted(found)]

    def bank(self, job):
        return self.known[2][job][0] if self.known else 0

    def done(self, job):
        return self.s.up(f"bank{self.jobs[job][0]}_filled", job)

    def full(self, job):
        return self.s.raw(f"bank{self.bank(job)}_filled"), (self.known[2][job][1] if self.known else 1)

    def drained(self, job):
        return self.s.up(f"bank{self.bank(job)}_drained", job)

    def emptied(self, job):
        return self.s.raw(f"bank{self.bank(job)}_drained"), (self.known[2][job][2] if self.known else 1)


def program(nc, I, outs, known=None):
    with ExitStack() as ctx:
        ctx.enter_context(nc.allow_non_contiguous_dma(reason="a few short parameter columns"))
        S = Signals(nc, ctx, known)
        K = Banks(S, known)

        def sb(name, shape):
            return ctx.enter_context(nc.sbuf_tensor(name, shape, F32))

        arena_offset = -(-nc.sbuf_base // 32) * 32
        R = nc.alloc_sbuf_tensor_at("arena", [P, NARENA], F32, offset=arena_offset)
        nc.sbuf_base = arena_offset + 4 * NARENA

        def rounded(name, off, n):
            return nc.alloc_sbuf_tensor_at(name, [P, n], F32R, offset=arena_offset + 4 * off)

        q_parts = rounded("q_parts", QT, 4 * TOK)[:, :].rearrange("p (h n) -> p h n", h=4)
        k_parts = rounded("k_parts", KT, 4 * NKEY * P)[:, :].rearrange("p (h n) -> p h n", h=4)
        split_buf = rounded("split_buf", SPLIT, 2 * 896)

        def at(off, *shape, parts=P, base=0):
            v = R[base:base + parts, off:off + int(np.prod(shape))]
            if len(shape) == 1:
                return v
            g = "abcd"[:len(shape)]
            return v.rearrange(f"p ({' '.join(g)}) -> p {' '.join(g)}", **dict(zip(g, shape)))

        ident = sb("ident", [P, P])
        sel = sb("sel", [2, 2, P])
        csil = sb("csil", [P, KD, 2])
        craw = sb("craw", [P, KD, 2])
        mcol = sb("mcol", [P, 2 * KD, 2])
        gpre = sb("gpre", [P, KD])
        negt = sb("negt", [P, TT])
        st = sb("st", [P, 80])
        lamv = sb("lamv", [P, 8])
        mhalf = sb("mhalf", [P, 8])
        mg = sb("mg", [P, 3])
        fwp = sb("fwp", [64, 4])
        hcw = sb("hcw", [P, 6, 4])
        psum = ctx.enter_context(nc.psum_tensor("psum", [P, 8 * 512], F32))
        bank = [psum[:, 512 * i:512 * (i + 1)] for i in range(8)]

        def score_view(group, n):
            return psum[:, 1536 * group:1536 * group + n]

        def B(job, n=512, parts=P):
            return bank[K.bank(job)][0:parts, 0:n]

        hT = at(HT, KD, TOK)
        oT = at(OT, KD, TOK)
        W = at(W0, 2, KD, WC)
        xs, spectrum_kept, gates_kept = outs["xs"], outs["spectrum_kept"], outs["gates_kept"]

        def rows(t):
            return slice(t, NT * P, NT) if t < NT else slice(NT * P, TOK)

        def stage_value(k):
            return S.raw("stage_done"), 4 * k

        passed = {}

        def stage_end(eng):
            eng.drain().then_inc(S.raw("stage_done"), 1)
            passed[id(eng)] = passed.get(id(eng), 0) + 1
            eng.wait_ge(*stage_value(passed[id(eng)]))

        def layer_end(eng):
            eng.drain().then_inc(S.raw("layer_finished"), 1)
            eng.wait_ge(S.raw("semaphores_cleared"), 1)
            eng.sem_inc(S.raw("layer_entered"), 1)

        block = ctx.enter_context(nc.Block())

        @block.sync
        def _(sp):
            def load(dst, src, name, key=None):
                sp.dma_start(dst, src).then_inc(*S.up(name, key, 16))

            sp.dma_start(ident[:, :], I["ident"]).then_inc(S.raw("constants"), 16)
            sp.dma_start(sel[:, :, :], I["sel"]).then_inc(S.raw("constants"), 16)
            sp.dma_start(craw[:, :, 0:1], I["c"].rearrange("o (k p) -> p k o", p=P)).then_inc(S.raw("constants"), 16)
            sp.dma_start(craw[:, :, 1:2], I["c_ctx"].rearrange("(o k p) -> p k o", p=P, o=1)).then_inc(S.raw("constants"), 16)
            sp.dma_start(negt[:, :], I["negt"]).then_inc(S.raw("constants"), 16)
            sp.dma_start(xs[0], I["x"]).then_inc(S.raw("x_copied"), 16)
            with sp.Fori(0, DEPTH) as l:
                def lay(name):
                    return I[name][bass.ds(l, 1)]

                def row(name, n=P):
                    return lay(name).to_broadcast([n, lay(name).shape[1]])

                turn = [0]

                def chunk():
                    name, j = c = STREAM[turn[0]]
                    if turn[0] >= 2:
                        sp.wait_ge(*K.full(LAST_JOB[STREAM[turn[0] - 2]]))
                    turn[0] += 1
                    if name in ("ada", "out"):
                        src, n = lay("ada_w" if name == "ada" else "w_out")[:, :, j * WC:(j + 1) * WC], WC
                    else:
                        c0, n = CHUNKS[name]
                        src = lay("w_in")[:, :, c0:c0 + n]
                    load(W[:, SLOT[c], :, 0:n], src.rearrange("o (k p) n -> p (o k) n", p=P),
                         f"weights{SLOT[c]}_loaded", c)

                sp.wait_ge(S.raw("x_copied"), 16)
                load(at(F_FEAT, TOK, parts=33), I["feats"], "filter_params")
                load(at(A_FW, 64, parts=33), lay("hy_fw1").rearrange("o k n -> (o k) n"), "filter_params")
                load(at(A_FW + 64, 64, parts=64), lay("hy_fw2").rearrange("o k n -> (o k) n"), "filter_params")
                load(at(A_FW3, 1024, parts=64), lay("hy_fw3").rearrange("o k n -> (o k) n"), "filter_params")
                load(fwp[:, 0:1], lay("hy_fb1").rearrange("o k -> k o"), "filter_params")
                load(fwp[:, 1:2], lay("hy_fb2").rearrange("o k -> k o"), "filter_params")
                load(fwp[:, 2:4], lay("hy_freq").rearrange("o f k -> k (o f)"), "filter_params")
                load(at(A_HBIAS, 512), row("hy_bias2"), "filter_params")
                load(at(A_DECAY, GW), row("hy_decay"), "filter_params")
                chunk()
                for s in range(2):
                    load(at(A_ADAB, 3072, parts=1, base=s), lay("ada_b"), "ada_params")
                load(at(A_NPOST, D), row("norm_post"), "ada_params")
                load(gpre[:, :], lay("norm_pre").rearrange("o (k p) -> p (o k)", p=P), "ada_params")
                load(at(TF, 4096), I["tab_f"], "transform_table")
                for _ in range(3):
                    chunk()
                for f in range(6):
                    load(hcw[:, f, 0:3], lay("hy_conv_w")[:, :, f * P:(f + 1) * P].rearrange("o t p -> p (o t)"), "conv_params")
                load(hcw[:, :, 3:4], lay("hy_conv_b").rearrange("o (f p) -> p f o", p=P), "conv_params")
                load(mg[:, 0:2], lay("mla_q_norm").rearrange("o (k p) -> p (o k)", p=P), "mla_gains")
                load(mg[:, 2:3], lay("mla_kv_norm").rearrange("o p -> p o"), "mla_gains")
                chunk()
                chunk()
                sp.wait_ge(*S.at("butterfly_pool", ("F", 1)))
                sp.wait_ge(*S.at("spectrum1_made"))
                sp.dma_start(spectrum_kept, at(HS, 4608)).then_inc(*S.up("spectrum1_kept", None, 16))
                chunk()
                chunk()
                for s in range(2):
                    for half in range(2):
                        sp.wait_ge(*K.emptied(("gate_row", s, half)))
                sp.dma_start(gates_kept, at(SGH, 2 * D)).then_inc(*S.up("gate_rows_kept", None, 16))
                sp.wait_ge(*stage_value(1))
                for t in range(TT):
                    if t >= 4:
                        sp.wait_ge(*K.full(("xT", t - 4, 1)))
                    load(at(XN + (t % 4) * D, D), xs[bass.ds(l, 1)][:, rows(t), :].rearrange("o p n -> (o p) n"),
                         f"x{t % 4}_loaded", t)
                load(at(TI, 4096), I["tab_i"], "inverse_table")
                chunk()
                sp.wait_ge(*S.at("product_vector", 0))
                sp.wait_ge(*S.at("product_pool", 0))
                sp.wait_ge(*S.at("spectrum1_kept"))
                load(at(HS, 4608), spectrum_kept, "spectrum1_back")
                chunk()
                sp.wait_ge(*stage_value(4))
                load(at(ROPE, NT, 192), I["rope"], "mla_params")
                load(at(WQB, 2, 384), lay("mla_wq_b").rearrange("o (k p) n -> p (o k) n", p=P), "mla_params")
                load(at(WKVB, 512), lay("mla_wkv_b").rearrange("o p n -> (o p) n"), "mla_params")
                load(at(KVGAIN, P), row("mla_kv_norm"), "mla_params")
                load(at(CKEY, P), I["cache_mla_ckv"][0][bass.ds(l, 1)].rearrange("o p n -> (o p) n"), "mla_params")
                load(at(CROPE, 32), I["cache_mla_krope"][0][bass.ds(l, 1)].rearrange("o p n -> (o p) n"), "mla_params")
                sp.wait_ge(*S.at("state_ready", "mla"))
                sp.dma_start(outs["new_mla_ckv"][0][bass.ds(l, 1)].rearrange("o p n -> (o p) n"),
                             at(CKVOUT, P)).then_inc(*S.up("state_stored", ("mla", 0), 16))
                sp.dma_start(outs["new_mla_krope"][0][bass.ds(l, 1)].rearrange("o p n -> (o p) n"),
                             at(ZB + 384, 32)).then_inc(*S.up("state_stored", "mla", 16))
                chunk()
                chunk()
                sp.wait_ge(*stage_value(5))
                for h in range(4):
                    load(at(WQB + 64 * h, 64), row("gqa_q_norm"), "gqa_params")
                for h in range(2):
                    load(at(WQB + 256 + 64 * h, 64), row("gqa_k_norm"), "gqa_params")
                load(at(CKEY, P), I["cache_gqa_k"][0][bass.ds(l, 1)].rearrange("o p h n -> (o p) (h n)"), "gqa_params")
                load(at(VV + CACHE * GW, P), I["cache_gqa_v"][0][bass.ds(l, 1)].rearrange("o p h n -> (o p) (h n)"), "gqa_params")
                sp.wait_ge(*S.at("state_ready", "gqa"))
                sp.wait_ge(*K.emptied(("proj", "gqa", NT)))
                sp.dma_start(outs["new_gqa_k"][0][bass.ds(l, 1)].rearrange("o p h n -> (o p) (h n)"),
                             at(ZB + 256, P)).then_inc(*S.up("state_stored", ("gqa", 0), 16))
                sp.dma_start(outs["new_gqa_v"][0][bass.ds(l, 1)].rearrange("o p h n -> (o p) (h n)"),
                             at(VV + PROMPT * GW, P)).then_inc(*S.up("state_stored", "gqa", 16))
                chunk()
                chunk()
                sp.wait_ge(*stage_value(6))
                load(at(WQB, 64), row("diff_subln"), "diff_params")
                for i, v in enumerate(("diff_lq1", "diff_lk1", "diff_lq2", "diff_lk2")):
                    load(at(WQB + 64 + 32 * i, 32), row(v), "diff_params")
                load(lamv[:, 4:6], row("lam_init"), "diff_params")
                load(at(VV + CACHE * GW, GW), I["cache_diff_v"][0][bass.ds(l, 1)].rearrange("o p h n -> (o p) (h n)"), "diff_params")
                for part in range(2):
                    if part == 1:
                        sp.wait_ge(*stage_value(7))
                    load(at(CKEY, P), I["cache_diff_k"][0][bass.ds(l, 1)][:, :, 2 * part:2 * part + 2, :]
                         .rearrange("o p h n -> (o p) (h n)"), f"diff{part}_cache")
                    sp.wait_ge(*S.at("state_ready", f"diff{part}"))
                    sp.dma_start(outs["new_diff_k"][0][bass.ds(l, 1)][:, :, 2 * part:2 * part + 2, :]
                                 .rearrange("o p h n -> (o p) (h n)"),
                                 at(ZB + P, P)).then_inc(*S.up("state_stored", f"diff{part}", 16))
                    if part == 0:
                        sp.wait_ge(*K.emptied(("gate", "diff", NT)))
                        sp.dma_start(outs["new_diff_v"][0][bass.ds(l, 1)].rearrange("o p h n -> (o p) (h n)"),
                                     at(VV + PROMPT * GW, GW)).then_inc(*S.up("state_stored", "diff_v", 16))
                chunk()
                chunk()
                sp.wait_ge(*stage_value(8))
                load(at(GR, 2 * D), gates_kept, "gate_rows_back")

                def store_x(t):
                    sp.wait_ge(*S.at("x_updated", t))
                    sp.dma_start(xs[bass.ds(l + 1, 1)][:, rows(t), :].rearrange("o p n -> (o p) n"),
                                 at(XR + (t % 3) * D, D)).then_inc(*S.up(f"x_stored{t % 3}", t, 16))

                for t in range(TT):
                    if t >= 3:
                        store_x(t - 3)
                        sp.wait_ge(*S.at(f"x_stored{t % 3}", t - 3))
                    load(at(XR + (t % 3) * D, D), xs[bass.ds(l, 1)][:, rows(t), :].rearrange("o p n -> (o p) n"),
                         f"xr{t % 3}_loaded", t)
                for t in range(TT - 3, TT):
                    store_x(t)
                for name in ("x_stored0", "x_stored1", "x_stored2", "state_stored"):
                    sp.wait_ge(*S.all(name))
                sp.wait_ge(S.raw("layer_finished"), 4)
                sp.sem_clear(S.counted_by_layer())
                sp.sem_clear(S.raw("layer_finished"))
                sp.sem_inc(S.raw("semaphores_cleared"), 1)
                sp.wait_ge(S.raw("layer_entered"), 4)
                sp.sem_clear(S.raw("semaphores_cleared"))
                sp.sem_clear(S.raw("layer_entered"))

        @block.tensor
        def _(pe):
            def claim(job, banks, drains=1):
                for w in K.claim(job, banks, drains):
                    pe.wait_ge(*w)
                return bank[banks[0]]

            def mm(out, lhsT, rhs, start=True, stop=True):
                return nc.tensor.matmul(out, lhsT, rhs, start=start, stop=stop)

            def flip(out, src):
                n = src.shape[0]
                return nc.tensor.transpose(out, src, ident[0:n, 0:n])

            pe.wait_ge(S.raw("constants"), 16 * N_CONST)
            pe.wait_ge(S.raw("silu_ready"), 3)
            with pe.Fori(0, DEPTH) as l:
                def weights(c, j=0):
                    pe.wait_ge(*S.at(f"weights{SLOT[c, j]}_loaded", (c, j)))

                def ada(j):
                    weights("ada", j)
                    ps = claim(("ada", j), K.next())
                    for k in range(KD):
                        last = mm(ps[0:2, :], csil[:, k, :], W[:, j % 2, k, :], k == 0, k == KD - 1)
                    last.then_inc(*K.done(("ada", j)))

                pe.wait_ge(*S.at("filter_params"))
                for i, (c, n) in enumerate(PARTS):
                    ps = claim(("f1", i), K.next())
                    mm(ps[0:64, 0:n], at(A_FW, 64, parts=33), at(F_FEAT + c, n, parts=33)
                       ).then_inc(*K.done(("f1", i)))
                pe.wait_ge(*S.at("sine", 1))
                for i, (c, n) in enumerate(PARTS):
                    ps = claim(("f2", i), K.next())
                    mm(ps[0:64, 0:n], at(A_FW + 64, 64, parts=64), at(F_ARG + c, n, parts=64)
                       ).then_inc(*K.done(("f2", i)))
                ada(0)
                pe.wait_ge(*S.at("sine", 2))
                tf = at(TF, 2 * NT, 2, P)
                ti = at(TI, 2 * NT, 2, P)
                eo = at(EO, TT, 3, GW)
                for o in (1, 0):
                    for t in range(TT):
                        ps = claim(("f3", o, t), K.next())
                        mm(ps[:, :], at(F_ARG + t * P, P, parts=64), at(A_FW3 + o * 512, 512, parts=64)
                           ).then_inc(*K.done(("f3", o, t)))
                    ada(1 if o else 4)
                    if o:
                        pe.wait_ge(*S.at("transform_table"))
                    pe.wait_ge(*S.at("filter_negated", o))
                    for a0 in range(4):
                        back = (4 - a0) % 4
                        if a0 == 2:
                            ada(2 if o else 5)
                        for p in range(2):
                            ps = claim(("FE", o, a0, p), K.next())
                            for ri in range(2):
                                terms = [(a, 0) for a in (a0, a0 + 4)] + [(a, 1 + ri) for a in (back, back + 4)]
                                for i, (a, kind) in enumerate(terms):
                                    last = mm(ps[:, ri * GW:(ri + 1) * GW], tf[:, 2 * a + p, ri, :],
                                              eo[:, a, kind, :], i == 0, i == 3)
                            last.then_inc(*K.done(("FE", o, a0, p)))
                    ps = claim(("FEp", o), K.next())
                    for ri in range(2):
                        for i, kind in enumerate((0, 1 + ri)):
                            last = mm(ps[:, ri * GW:(ri + 1) * GW], tf[:, 0, ri, :], eo[:, NT, kind, :], i == 0, i == 1)
                    last.then_inc(*K.done(("FEp", o)))
                    if o:
                        ada(3)
                mod = at(A_MOD, 3072, parts=2)
                for j in range(4):
                    pe.wait_ge(*K.emptied(("ada", j)))
                ps = claim(("modT",), K.next())
                for m in range(2 * KD):
                    last = flip(ps[:, 2 * m:2 * m + 2], mod[:, m * P:(m + 1) * P])
                last.then_inc(*K.done(("modT",)))
                for s in range(2):
                    for half in range(2):
                        pe.wait_ge(*K.emptied(("ada", 4 + half)))
                        ps = claim(("gate_row", s, half), K.next())
                        mm(ps[:, :], sel[:, s, :], mod[:, 2 * D + half * 512:2 * D + (half + 1) * 512]
                           ).then_inc(*K.done(("gate_row", s, half)))
                stage_end(pe)

                for t in range(TT):
                    pe.wait_ge(*S.at("x_normed", t))
                    for half in range(2):
                        ps = claim(("xT", t, half), K.next())
                        for k in range(4):
                            last = flip(ps[:, k * P:(k + 1) * P], at(XN + (t % 4) * D + (half * 4 + k) * P, P))
                        last.then_inc(*K.done(("xT", t, half)))
                stage_end(pe)

                def to_tokens(f):
                    for g in range(3):
                        if g == 0:
                            pe.wait_ge(*S.at("taps", f))
                        ps = claim(("uT", f, g), K.next())
                        for i in range(1 if g == 2 else 4):
                            last = flip(ps[:, i * P:(i + 1) * P], at(CU + (f % 2) * TOK + (4 * g + i) * P, P))
                        last.then_inc(*K.done(("uT", f, g)))

                for f in range(6):
                    c = "hy0" if f < 4 else "hy1"
                    weights(c)
                    for i, (tok, n) in enumerate(PARTS):
                        ps = claim(("u", f, i), K.next())
                        for k in range(KD):
                            last = mm(ps[:, 0:n], W[:, SLOT[c, 0], k, (f % 4) * P:(f % 4 + 1) * P],
                                      hT[:, k, tok:tok + n], k == 0, k == KD - 1)
                        last.then_inc(*K.done(("u", f, i)))
                    if f >= 1:
                        to_tokens(f - 1)

                def project(grp, kind, t, c, c0, n, drains=1):
                    job = (kind, grp, t)
                    ps = claim(job, K.next(), drains)
                    for k in range(KD):
                        last = mm(ps[:, 0:n], hT[:, k, t * P:(t + 1) * P], W[:, SLOT[c, 0], k, c0:c0 + n],
                                  k == 0, k == KD - 1)
                    last.then_inc(*K.done(job))

                for t in range(2):
                    project("hy", "gate", t, "hy1", 256, GW)
                to_tokens(5)
                stage_end(pe)

                zv = at(XV, TT, 3, GW)
                for o in range(2):
                    for a0 in range(4):
                        if o == 1:
                            pe.wait_ge(*K.emptied(("Y", 0, a0 // 2)))
                            pe.wait_ge(*K.emptied(("Y", 0, 2 + a0 // 2)))
                        for p in range(2):
                            ps = claim(("Z", o, a0, p), K.next())
                            for ri in range(2):
                                for i, a in enumerate((a0, a0 + 4)):
                                    last = mm(ps[:, ri * GW:(ri + 1) * GW], tf[:, 2 * a + p, ri, :],
                                              zv[:, a, 2, :], i == 0, i == 1)
                            last.then_inc(*K.done(("Z", o, a0, p)))
                    if o == 1:
                        pe.wait_ge(*K.emptied(("Yp", 0)))
                    ps = claim(("Zp", o), K.next())
                    for ri in range(2):
                        last = mm(ps[:, ri * GW:(ri + 1) * GW], tf[:, 0, ri, :], zv[:, NT, 2, :])
                    last.then_inc(*K.done(("Zp", o)))
                    if o == 0:
                        for t in range(2, TT):
                            project("hy", "gate", t, "hy1", 256, GW)
                        pe.wait_ge(*S.at("inverse_table"))
                    else:
                        weights("mla_gate")
                        for t in range(TT):
                            project("mla", "gate", t, "mla_gate", 0, GW)
                    pe.wait_ge(*S.at("butterfly_vector", ("G", o)))
                    pe.wait_ge(*S.at("butterfly_pool", ("G", o)))
                    G = at(B3, 4, 2, 2, GW)
                    for i in range(4):
                        ps = claim(("Y", o, i), K.next())
                        for a in (2 * i, 2 * i + 1):
                            terms = [(p, ri) for p in range(2) for ri in range(2)]
                            for n, (p, ri) in enumerate(terms):
                                last = mm(ps[:, (a % 2) * GW:(a % 2 + 1) * GW], ti[:, 2 * a + p, ri, :],
                                          G[:, a % 4, p, ri, :], n == 0, n == 3)
                        last.then_inc(*K.done(("Y", o, i)))
                    pe.wait_ge(*S.at("product_prompt", o))
                    ps = claim(("Yp", o), K.next())
                    for ri in range(2):
                        last = mm(ps[:, 0:GW], ti[:, 0, ri, :], at(B3 + 4096 + ri * GW, GW), ri == 0, ri == 1)
                    last.then_inc(*K.done(("Yp", o)))

                def out_tile(grp, t, src, banks):
                    pe.wait_ge(*S.at("gated", (grp, t)))
                    ps = claim(("oT", grp, t), banks)
                    for i in range(src.shape[1] // P):
                        last = flip(ps[:, i * P:(i + 1) * P], src[:, i * P:(i + 1) * P])
                    last.then_inc(*K.done(("oT", grp, t)))

                for t in range(TT):
                    out_tile("hy", t, zv[:, t, 2, :], K.next())
                stage_end(pe)

                def attention(grp):
                    two = NMAPS[grp] == 2
                    units, heads = UNITS[grp], HEADS[grp]
                    NU, NH = len(units), len(heads)

                    def scores(i, maps=(0,)):
                        t, h = units[i]
                        for s in maps:
                            g = s if two else i % 2
                            claim(("S", grp, i, s), [3 * g, 3 * g + 1, 3 * g + 2])
                            m = 2 * heads.index(h) + s if two else h
                            qs, k0 = slice(t * P, (t + 1) * P), PROMPT * P if t == NT else 0
                            for j, (c, n) in enumerate(((0, P),) if t == NT else PARTS):
                                out, ks = bank[3 * g + j][:, 0:n], slice(k0 + c, k0 + c + n)
                                if grp == "mla":
                                    last = mm(out, at(QT + m * TOK + t * P, P, parts=96),
                                              at(KT + m * NKEY * P + k0 + c, n, parts=96))
                                elif grp == "gqa":
                                    mm(out, q_parts[:, m, qs], k_parts[:, h - h % 2, ks], True, False)
                                    last = mm(out, q_parts[0:64, m, qs], k_parts[0:64, h - h % 2 + 1, ks], False, True)
                                else:
                                    last = mm(out, q_parts[0:96, m, qs], k_parts[0:96, m, ks])
                            last.then_inc(*K.done(("S", grp, i, s)))

                    def turn_one(i):
                        t, _ = units[i]
                        pe.wait_ge(*K.emptied(("S", grp, i, 0)))
                        g = i % 2
                        claim(("T", grp, i), [3 * g, 3 * g + 1, 3 * g + 2], 1 if t == NT else 2)
                        for j in range(n_keys(t)):
                            last = flip(bank[3 * g + j // 4][:, (j % 4) * P:(j % 4 + 1) * P],
                                        at(PB + (i % 2) * TOK + j * P, P))
                        last.then_inc(*K.done(("T", grp, i)))

                    def two_maps(i):
                        nb = (n_keys(units[i][0]) + 3) // 4 if i >= 0 else 0
                        if nb:
                            pe.wait_ge(*S.at("combined", (grp, i)))
                        for b in range(3):
                            if b < nb:
                                ps = claim(("T", grp, i, b), [6])
                                for j in range(4 * b, min(4 * b + 4, n_keys(units[i][0]))):
                                    last = flip(ps[:, (j % 4) * P:(j % 4 + 1) * P], at(PB + (i % 2) * TOK + j * P, P))
                                last.then_inc(*K.done(("T", grp, i, b)))
                                if b == 0:
                                    claim(("O", grp, i), [7])
                                else:
                                    values(i, 4 * b - 4, 4 * b)
                            if b < 2 and i + 2 < NU:
                                scores(i + 2, (b,))
                        if nb:
                            values(i, 4 * nb - 4, n_keys(units[i][0]))

                    def values(i, j0, j1):
                        t, h = units[i]
                        vc = 64 * (h // 2) if grp == "gqa" else 64 * h
                        ps = bank[7 if two else 6]
                        nk = n_keys(t)
                        pe.wait_ge(*K.emptied(("T", grp, i, j0 // 4) if two else ("T", grp, i)))
                        for j in range(j0, j1):
                            kt = PROMPT if t == NT else j
                            last = mm(ps[:, 0:64], at(PT + (i % 2) * TOK + j * P, P),
                                      at(VV + kt * GW + vc, 64), j == 0, j == nk - 1)
                        if j1 == nk:
                            last.then_inc(*K.done(("O", grp, i)))

                    lag = 2
                    for i in range(NU + lag + 1):
                        if two and i == 0:
                            scores(0, (0, 1))
                        if not two and i < NU:
                            scores(i)
                        n = i - lag - 1
                        tile_done = n >= 0 and n % NH == NH - 1
                        if two and tile_done:
                            out_tile(grp, units[n][0], at(OB + (units[n][0] % 2) * GW, 64 * NH), [6])
                        if two and i <= NU:
                            two_maps(i - 1)
                        if not two and 1 <= i <= NU:
                            turn_one(i - 1)
                        if not two and lag <= i < NU + lag:
                            claim(("O", grp, i - lag), [6])
                            values(i - lag, 0, n_keys(units[i - lag][0]))
                        if not two and tile_done:
                            t = units[n][0]
                            out_tile(grp, t, at(OB + (t % 2) * GW, 64 * NH), [7])

                def gates(grp, c):
                    weights(c)
                    for t in range(TT):
                        project(grp, "gate", t, c, 0, CHUNKS[c][1])

                def mla_latent(t):
                    pe.wait_ge(*S.at("latent", t))
                    ps = claim(("cT", t), K.next())
                    if t < TT:
                        for i in range(3):
                            last = flip(ps[:, i * P:(i + 1) * P], at(ZB + (t % 2) * WC + i * P, P))
                    else:
                        last = flip(ps[:, 2 * P:3 * P], at(CKEY, P))
                    last.then_inc(*K.done(("cT", t)))

                def mla_expand(t):
                    pe.wait_ge(*K.emptied(("cT", t)))
                    if t < TT:
                        ps = claim(("q", t), K.next())
                        for k in range(2):
                            last = mm(ps[:, 0:384], at(CT + k * P, P), at(WQB + k * 384, 384), k == 0, k == 1)
                        last.then_inc(*K.done(("q", t)))
                    ps = claim(("kv", t), K.next())
                    mm(ps[:, :], at(CT + 2 * P, P), at(WKVB, 512)).then_inc(*K.done(("kv", t)))

                def mla_turn(t):
                    if t < TT:
                        pe.wait_ge(*S.at("q_roped", t))
                        ps = claim(("qT", t), K.next())
                        for h in range(MLA_HEADS):
                            last = flip(ps[0:96, h * P:(h + 1) * P], at(QS + h * 96, 96))
                        last.then_inc(*K.done(("qT", t)))
                    pe.wait_ge(*K.emptied(("kv", t)))
                    pe.wait_ge(*S.at("k_rope_spread", t))
                    ps = claim(("kT", t), K.next())
                    for h in range(MLA_HEADS):
                        last = flip(ps[0:96, h * P:(h + 1) * P], at(QS + 384 + h * 96, 96))
                    last.then_inc(*K.done(("kT", t)))

                weights("mla")
                pe.wait_ge(*S.at("mla_params"))
                for i in range(TT + 3):
                    if 1 <= i <= TT + 1:
                        mla_latent(i - 1)
                    if i < TT:
                        project("mla", "proj", i, "mla", 0, 416)
                    if 2 <= i <= TT + 2:
                        mla_turn(i - 2)
                    if 1 <= i <= TT + 1:
                        mla_expand(i - 1)
                pe.wait_ge(*K.emptied(("qT", NT)))
                pe.wait_ge(*K.emptied(("kT", TT)))
                attention("mla")
                stage_end(pe)

                def parts_turned(grp, t):
                    pe.wait_ge(*S.at("split", (grp, t)))
                    src = split_buf[:, (t % 2) * 896:(t % 2) * 896 + SPLIT_W[grp]].bitcast(F32)
                    rows = 128 if grp == "gqa" else 96
                    if t < TT:
                        ps = claim(("qT", grp, t), K.next())
                        for i in range(4):
                            last = flip(ps[0:rows, i * P:(i + 1) * P], src[:, i * rows:(i + 1) * rows])
                        last.then_inc(*K.done(("qT", grp, t)))
                    ps = claim(("kT", grp, t), K.next())
                    for i in range(4):
                        c, n = (512 + 192 * (i // 2) + 128 * (i % 2), 128 - 64 * (i % 2)) if grp == "gqa" else \
                            (384 + i * 96, 96)
                        last = flip(ps[0:n, i * P:(i + 1) * P], src[:, c:c + n])
                    last.then_inc(*K.done(("kT", grp, t)))

                for grp in ("gqa", "diff0", "diff1"):
                    chunk_name = grp[:4]
                    if grp != "diff1":
                        weights(chunk_name)
                        pe.wait_ge(*S.at(f"{chunk_name}_params"))
                    for i in range(TT + 1):
                        if i < TT and grp == "gqa":
                            project(grp, "proj", i, grp, 0, 512)
                        elif i < TT:
                            ps = claim(("proj", grp, i), K.next())
                            for k in range(KD):
                                w = W[:, SLOT["diff", 0], k, :].rearrange("p (a b n) -> p a b n", a=2, b=2)
                                last = mm(ps[:, 0:256], hT[:, k, i * P:(i + 1) * P], w[:, :, int(grp[4]), :],
                                          k == 0, k == KD - 1)
                            last.then_inc(*K.done(("proj", grp, i)))
                        if i >= 1:
                            parts_turned(grp, i - 1)
                    parts_turned(grp, TT)
                    if grp != "diff1":
                        gates(chunk_name, "gqa_gate" if grp == "gqa" else "diff_vg")
                        pe.wait_ge(*K.emptied(("gate", chunk_name, NT)))
                    pe.wait_ge(*K.emptied(("qT", grp, NT)))
                    pe.wait_ge(*K.emptied(("kT", grp, NT)))
                    pe.wait_ge(*K.emptied(("kT", grp, TT)))
                    attention(grp)
                    stage_end(pe)

                for half in range(2):
                    weights("out", half)
                for t in range(TT):
                    for half in range(2):
                        ps = claim(("y", t, half), K.next())
                        for k in range(KD):
                            last = mm(ps[:, :], oT[:, k, t * P:(t + 1) * P], W[:, half, k, :], k == 0, k == KD - 1)
                        last.then_inc(*K.done(("y", t, half)))
                stage_end(pe)
                layer_end(pe)

        @block.scalar
        def _(act):
            def link(ins):
                ins.then_inc(*S.up("scalar_step"))
                act.wait_ge(*S.now("scalar_step"))

            act.wait_ge(S.raw("constants"), 16 * N_CONST)
            nc.scalar.activation(csil[:, :, :], craw[:, :, :], ACT.Tanh, scale=0.5).then_inc(S.raw("silu_ready"), 1)
            with act.Fori(0, DEPTH) as l:
                act.wait_ge(*S.at("filter_params"))
                link(nc.scalar.activation(at(A_DECAY, GW), at(A_DECAY, GW), ACT.Abs))
                for t in range(TT):
                    nc.scalar.activation(at(A_DEC + t * GW, GW), at(A_DECAY, GW), ACT.Exp, scale=negt[:, t:t + 1]
                                         ).then_inc(*S.up("decay", t))
                for n in (1, 2):
                    act.wait_ge(*S.at("angle", n))
                    nc.scalar.activation(at(F_ARG, TOK, parts=64), at(F_ARG, TOK, parts=64), ACT.Sin
                                         ).then_inc(*S.up("sine", n))
                for o in (1, 0):
                    if o == 0:
                        act.wait_ge(*S.at("butterfly_sums", ("F", 1)))
                        act.wait_ge(*S.at("butterfly_diffs", ("F", 1)))
                        act.wait_ge(*S.at("spectrum1_made"))
                    for a0 in range(4):
                        for p in range(2):
                            job = ("FE", o, a0, p)
                            act.wait_ge(*K.full(job))
                            nc.scalar.mul(at(B2 + (a0 * 2 + p) * 512, 512), B(job), 1.0 / N_SAMPLE
                                          ).then_inc(*K.drained(job))
                    act.wait_ge(*K.full(("FEp", o)))
                    nc.scalar.mul(at(B2 + 4096, 512), B(("FEp", o)), 1.0 / N_PROMPT).then_inc(*K.drained(("FEp", o)))
                stage_end(act)

                for t in range(TT + 2):
                    if t < TT:
                        act.wait_ge(*S.at(f"x{t % 4}_loaded", t))
                        if t >= 1:
                            act.wait_ge(*S.at("x_squares", t - 1))
                        nc.scalar.activation(at(B3, D), at(XN + (t % 4) * D, D), ACT.Square,
                                             accum_out=st[:, t:t + 1]).then_inc(*S.up("x_squares", t))
                    if t >= 2:
                        job, s = ("xT", t - 2, 0), int(t - 2 == NT)
                        act.wait_ge(*K.full(job))
                        for k in range(4):
                            last = nc.scalar.activation(hT[:, k, (t - 2) * P:(t - 1) * P], B(job)[:, k * P:(k + 1) * P],
                                                        ACT.Identity, scale=mcol[:, KD + k, s:s + 1],
                                                        bias=mcol[:, k, s:s + 1])
                        last.then_inc(*K.drained(job))
                stage_end(act)

                act.wait_ge(*S.at("conv_params"))
                for f in range(6):
                    u = U0 + (f % 2) * UW
                    if f >= 2:
                        act.wait_ge(*S.at("taps", f - 2))
                    for i in range(3):
                        job = ("u", f, i)
                        act.wait_ge(*K.full(job))
                        dst = at(u + (1 + 4 * i) * P, 512) if i < 2 else at(u + 10 * P + 1, P)
                        nc.scalar.copy(dst, B(job, 512 if i < 2 else P)).then_inc(*K.drained(job))
                        act.wait_ge(*K.emptied(job))
                    if f >= 2:
                        act.wait_ge(*K.full(("uT", f - 2, 2)))
                    nc.scalar.activation(at(CU + (f % 2) * TOK, D), at(u + P, D), ACT.Identity,
                                         scale=hcw[:, f, 1:2], bias=hcw[:, f, 3:4])
                    nc.scalar.activation(at(CU + (f % 2) * TOK + D, P), at(u + 10 * P + 1, P), ACT.Identity,
                                         scale=hcw[:, f, 1:2], bias=hcw[:, f, 3:4]).then_inc(*S.up("middle_tap", f))
                    if f >= 1:
                        drain_uT = f - 1
                        for g in (0,):
                            job = ("uT", drain_uT, g)
                            act.wait_ge(*K.full(job))
                            nc.scalar.copy(at(XV, TT, 768)[:, 0:4, drain_uT * P:(drain_uT + 1) * P],
                                           B(job).rearrange("p (a n) -> p a n", a=4)).then_inc(*K.drained(job))
                def half_tanh(grp, t, c0=0):
                    job = ("gate", grp, t)
                    act.wait_ge(*K.full(job))
                    if t >= 2:
                        act.wait_ge(*K.emptied(("gate", grp, t - 2)))
                    dst = (GATE_T if grp in ("hy", "mla") else OB) + (t % 2) * GW
                    nc.scalar.activation(at(dst, GW), B(job)[:, c0:c0 + GW], ACT.Tanh, scale=0.5
                                         ).then_inc(*S.up("half_tanh", (grp, t)))

                for t in range(2):
                    half_tanh("hy", t)
                job = ("uT", 5, 0)
                act.wait_ge(*K.full(job))
                nc.scalar.copy(at(XV, TT, 768)[:, 0:4, 5 * P:6 * P],
                               B(job).rearrange("p (a n) -> p a n", a=4)).then_inc(*K.drained(job))
                stage_end(act)

                for o in range(2):
                    if o == 1:
                        act.wait_ge(*K.full(("Y", 0, 3)))
                    for a0 in range(4):
                        job = ("Z", o, a0, 0)
                        act.wait_ge(*K.full(job))
                        nc.scalar.copy(at(B2 + (a0 * 2) * 512, 512), B(job)).then_inc(*K.drained(job))
                    act.wait_ge(*K.full(("Zp", o)))
                    nc.scalar.copy(at(B2 + 4096, 512), B(("Zp", o))).then_inc(*K.drained(("Zp", o)))
                    for t in range(0 if o else 2, TT):
                        half_tanh("mla" if o else "hy", t)

                def drain_oT(grp, t):
                    job, f, n = ("oT", grp, t), OUT_TILE[grp], 1 if grp[:4] == "diff" else 2
                    act.wait_ge(*K.full(job))
                    nc.scalar.copy(oT[:, f:f + n, t * P:(t + 1) * P],
                                   B(job, n * P).rearrange("p (a n) -> p a n", a=n)).then_inc(*K.drained(job))

                for t in range(TT):
                    drain_oT("hy", t)
                stage_end(act)

                def attention(grp):
                    two = NMAPS[grp] == 2
                    units = UNITS[grp]
                    NU, NH = len(units), len(HEADS[grp])
                    scale = DK[grp] ** -0.5

                    def turned(i, batches=(0,)):
                        t, _ = units[i]
                        if i >= 2:
                            act.wait_ge(*K.full(("O", grp, i - 2)))
                        pt = PT + (i % 2) * TOK
                        if two:
                            for b in batches:
                                if 4 * b >= n_keys(t):
                                    break
                                job, n = ("T", grp, i, b), min(512, n_keys(t) * P - 512 * b)
                                act.wait_ge(*K.full(job))
                                nc.scalar.copy(at(pt + 512 * b, n), B(job, n)).then_inc(*K.drained(job))
                        elif t < NT:
                            job = ("T", grp, i)
                            act.wait_ge(*K.full(job))
                            nc.scalar.copy(at(pt, 512), B(job)).then_inc(*K.drained(job))

                    def exp(i, s):
                        t, _ = units[i]
                        job = ("S", grp, i, s)
                        act.wait_ge(*S.at("neg_max", (grp, i, s)))
                        slot = 2 if s == 1 else i % 2
                        if s == 1 and i >= 1:
                            act.wait_ge(*S.at("combined", (grp, i - 1)))
                        elif i >= 2:
                            act.wait_ge(*K.full(("T", grp, i - 2, (n_keys(units[i - 2][0]) - 1) // 4)
                                                if two else ("T", grp, i - 2)))
                        nk = n_keys(t) * P
                        col = 16 * (i % 4) + 8 * s
                        nc.scalar.activation(at(PB + slot * TOK, nk), score_view(s if two else i % 2, nk), ACT.Exp,
                                             bias=st[:, col + 1:col + 2], scale=scale,
                                             accum_out=st[:, col + 2:col + 3]).then_inc(*K.drained(job))

                    lag = 2
                    for i in range(NU + lag + 1):
                        if two and i < NU:
                            exp(i, 0)
                        n = i - lag - 1
                        tile_done = n >= 0 and n % NH == NH - 1
                        if two and tile_done:
                            drain_oT(grp, units[n][0])
                        if 1 <= i <= NU:
                            turned(i - 1)
                        if i < NU:
                            exp(i, 1 if two else 0)
                        if two and 1 <= i <= NU:
                            turned(i - 1, (1, 2))
                        if not two and tile_done:
                            drain_oT(grp, units[n][0])

                for i in range(TT + 3):
                    if i < TT:
                        job, z = ("proj", "mla", i), ZB + (i % 2) * WC
                        act.wait_ge(*K.full(job))
                        if i >= 2:
                            act.wait_ge(*K.full(("cT", i - 2)))
                            act.wait_ge(*S.at("k_rope_spread", i - 2))
                        nc.scalar.copy(at(z, 416), B(job, 416)).then_inc(*K.drained(job))
                        act.wait_ge(*K.emptied(job))
                        if i >= 1:
                            act.wait_ge(*S.at("latent_squares", i - 1))
                        nc.scalar.activation(at(PT, GW), at(z, GW), ACT.Square, accum_out=st[:, 4 * (i % 2):4 * (i % 2) + 1])
                        nc.scalar.activation(at(PT + GW, P), at(z + GW, P), ACT.Square,
                                             accum_out=st[:, 4 * (i % 2) + 1:4 * (i % 2) + 2]).then_inc(*S.up("latent_squares", i))
                    if 2 <= i <= TT + 1:
                        job, t = ("qT", i - 2), i - 2
                        if t < TT:
                            act.wait_ge(*K.full(job))
                            nc.scalar.copy(at(QT, MLA_HEADS, TOK, parts=96)[:, :, t * P:(t + 1) * P],
                                           B(job, parts=96).rearrange("p (h n) -> p h n", h=MLA_HEADS)).then_inc(*K.drained(job))
                    if 1 <= i <= TT + 1:
                        t = i - 1
                        if t < TT:
                            job = ("q", t)
                            act.wait_ge(*K.full(job))
                            if t >= 1:
                                act.wait_ge(*K.full(("qT", t - 1)))
                            nc.scalar.copy(at(QS, 384), B(job, 384)).then_inc(*K.drained(job))
                        job = ("kv", t)
                        act.wait_ge(*K.full(job))
                        if t >= 1:
                            act.wait_ge(*K.full(("kT", t - 1)))
                        kt = CACHE if t == TT else key_tile(t)
                        kv = B(job).rearrange("p (h n) -> p h n", h=MLA_HEADS)
                        nc.scalar.copy(at(VV + kt * GW, MLA_HEADS, 64), kv[:, :, 64:128])
                        nc.scalar.copy(at(QS + 384, MLA_HEADS, 96)[:, :, 0:64], kv[:, :, 0:64]).then_inc(*K.drained(job))
                act.wait_ge(*S.at("state_stored", "mla"))
                attention("mla")
                stage_end(act)

                for grp in ("gqa", "diff0", "diff1"):
                    rows, pn = (128, 512) if grp == "gqa" else (96, 256)

                    def parts_turned(t):
                        if t < TT:
                            job = ("qT", grp, t)
                            act.wait_ge(*K.full(job))
                            nc.scalar.copy(q_parts[0:rows, :, t * P:(t + 1) * P],
                                           B(job, parts=rows).rearrange("p (a n) -> p a n", a=4)).then_inc(*K.drained(job))
                        job, kt = ("kT", grp, t), CACHE if t == TT else key_tile(t)
                        act.wait_ge(*K.full(job))
                        if grp == "gqa":
                            ps = B(job).rearrange("p (a b n) -> p a b n", a=2, b=2)
                            kp = k_parts[:, :, kt * P:(kt + 1) * P].rearrange("p (a b) n -> p a b n", a=2)
                            nc.scalar.copy(kp[:, :, 0, :], ps[:, :, 0, :])
                            nc.scalar.copy(kp[0:64, :, 1, :], ps[0:64, :, 1, :]).then_inc(*K.drained(job))
                        else:
                            nc.scalar.copy(k_parts[0:96, :, kt * P:(kt + 1) * P],
                                           B(job, parts=96).rearrange("p (a n) -> p a n", a=4)).then_inc(*K.drained(job))

                    if grp == "gqa":
                        act.wait_ge(*S.at("gqa_params"))
                    for i in range(TT + 1):
                        if i < TT:
                            job, z = ("proj", grp, i), ZB + (i % 2) * WC
                            act.wait_ge(*K.full(job))
                            if i >= 2:
                                act.wait_ge(*S.at("split", (grp, i - 2)))
                            nz = 384 if grp == "gqa" else 256
                            ins = nc.scalar.copy(at(z, nz), B(job)[:, 0:nz])
                            if grp == "gqa":
                                ins = nc.scalar.copy(at(VV + key_tile(i) * GW, P), B(job)[:, 384:512])
                            ins.then_inc(*K.drained(job))
                        if i >= 1:
                            parts_turned(i - 1)
                    parts_turned(TT)
                    if grp == "gqa":
                        for t in range(TT):
                            half_tanh(grp, t)
                    if grp == "diff0":
                        for t in range(TT):
                            act.wait_ge(*K.full(("gate", "diff", t)))
                            nc.scalar.copy(at(VV + key_tile(t) * GW, GW), B(("gate", "diff", t))[:, 0:GW])
                            half_tanh("diff", t, GW)
                        act.wait_ge(*S.at("lambda_sums"))
                        nc.scalar.activation(lamv[:, 2:4], lamv[:, 0:2], ACT.Exp).then_inc(*S.up("lambda_exps"))
                    act.wait_ge(*S.at("state_stored", "diff_v" if grp == "diff0" else grp))
                    attention(grp)
                    stage_end(act)

                for t in range(TT):
                    for half in range(2):
                        job = ("y", t, half)
                        act.wait_ge(*K.full(job))
                        if t + half >= 1:
                            act.wait_ge(*S.at("out_squares", (t, 0) if half else (t - 1, 1)))
                        if t >= 2:
                            act.wait_ge(*K.emptied(("y", t - 2, 1)))
                        nc.scalar.activation(at(YN + 2 * D, 512), B(job), ACT.Square,
                                             accum_out=st[:, 8 * (t % 2) + half:8 * (t % 2) + half + 1]
                                             ).then_inc(*S.up("out_squares", (t, half)))
                stage_end(act)
                layer_end(act)

        @block.vector
        def _(v):
            def link(ins, name="vector_step", key=None):
                ins.then_inc(*S.up(name, key))
                v.wait_ge(*S.now(name))

            def tt(out, a, b, op):
                return nc.vector.tensor_tensor(out, a, b, op)

            def rstd(key, *parts):
                for x, n in parts:
                    last = nc.vector.tensor_scalar(x, x, 1.0 / n, EPS, ALU.mult, ALU.add)
                last.then_inc(*S.up("variance", key))
                v.wait_ge(*S.at("inverse_root", key))

            v.wait_ge(S.raw("silu_ready"), 1)
            nc.vector.scalar_tensor_tensor(csil[:, :, :], csil[:, :, :], 1.0, craw[:, :, :], ALU.add, ALU.mult
                                           ).then_inc(S.raw("silu_ready"), 1)
            v.wait_ge(S.raw("silu_ready"), 2)
            nc.vector.tensor_scalar(csil[:, :, :], csil[:, :, :], 0.5, None, ALU.mult).then_inc(S.raw("silu_ready"), 1)
            with v.Fori(0, DEPTH) as l:
                mod = at(A_MOD, 3072, parts=2)

                def add_ada_bias(j):
                    v.wait_ge(*S.at("ada_params"))
                    v.wait_ge(*K.full(("ada", j)))
                    tt(mod[:, j * 512:(j + 1) * 512], B(("ada", j), parts=2),
                       at(A_ADAB + j * 512, 512, parts=2), ALU.add).then_inc(*K.drained(("ada", j)))

                v.wait_ge(*S.at("filter_params"))
                x, kk = at(F_ARG, TOK, parts=64), at(F_K, TOK, parts=64)
                for n in (1, 2):
                    for i, (c, w) in enumerate(PARTS):
                        job = (f"f{n}", i)
                        v.wait_ge(*K.full(job))
                        if n == 2 and i == 0:
                            v.wait_ge(*K.full(("f2", 2)))
                        nc.vector.tensor_scalar(at(F_ARG + c, w, parts=64), B(job, w, 64), fwp[:, n - 1:n],
                                                fwp[:, n + 1:n + 2], ALU.add, ALU.mult).then_inc(*K.drained(job))
                        v.wait_ge(*K.emptied(job))
                    link(nc.vector.tensor_scalar(kk, x, 1.0 / TWO_PI, MAGIC, ALU.mult, ALU.add))
                    link(nc.vector.tensor_scalar(kk, kk, MAGIC, None, ALU.subtract))
                    for part in (PI_A, PI_B, PI_C):
                        link(nc.vector.scalar_tensor_tensor(x, kk, -part, x, ALU.mult, ALU.add))
                    nc.vector.tensor_scalar(x, x, -PI_SAFE, PI_SAFE, ALU.max, ALU.min).then_inc(*S.up("angle", n))

                def butterfly(key, src, mid, dst, sign):
                    E, M, X = at(src, 4, D), at(mid, 4, D), at(dst, 4, D)
                    link(tt(M[:, 0:2, :], E[:, 0:2, :], E[:, 2:4, :], ALU.add), "butterfly_sums", key)
                    if src == dst:
                        v.wait_ge(*S.at("butterfly_diffs", key))
                    tt(X[:, 0, :], M[:, 0, :], M[:, 1, :], ALU.add)
                    link(tt(X[:, 2, :], M[:, 0, :], M[:, 1, :], ALU.subtract), "butterfly_vector", key)

                add_ada_bias(0)
                eo = at(EO, TT, 3, GW)
                for o in (1, 0):
                    for t in range(TT):
                        job = ("f3", o, t)
                        v.wait_ge(*K.full(job))
                        v.wait_ge(*S.at("decay", t))
                        if o == 0 and t == 0:
                            v.wait_ge(*K.full(("FEp", 1)))
                        tt(eo[:, t, 0:2, :], B(job).rearrange("p (a n) -> p a n", a=2),
                           at(A_DEC + t * GW, GW).unsqueeze(1).to_broadcast([P, 2, GW]), ALU.mult
                           ).then_inc(*K.drained(job))
                        if t in (0, NT):
                            v.wait_ge(*K.emptied(job))
                            nc.vector.memset(eo[0:1, t, 1, :], 0.0).then_inc(*S.up("lag0_cleared", (o, t)))
                    for j in ((1, 2) if o else (4, 5)):
                        add_ada_bias(j)
                    for a0 in range(4):
                        for p in range(2):
                            v.wait_ge(*K.emptied(("FE", o, a0, p)))
                    E = at(B2, 4, 2, 2, GW)
                    bias = at(A_HBIAS + o * GW, GW)
                    for p in range(2):
                        link(nc.vector.scalar_tensor_tensor(E[:, 0, p, 0, :], bias, 1.0 / N_SAMPLE, E[:, 0, p, 0, :],
                                                            ALU.mult, ALU.add), "bias_added", (o, p))
                    if o == 0:
                        v.wait_ge(*S.at("spectrum1_kept"))
                    butterfly(("F", o), B2, B3, HS, -1)
                    v.wait_ge(*K.emptied(("FEp", o)))
                    nc.vector.scalar_tensor_tensor(at(HS + 4096, GW), bias, 1.0 / N_PROMPT, at(B2 + 4096, GW),
                                                   ALU.mult, ALU.add)
                    nc.vector.tensor_copy(at(HS + 4096 + GW, GW), at(B2 + 4096 + GW, GW)
                                          ).then_inc(*S.up(f"spectrum{o}_made"))
                    if o:
                        add_ada_bias(3)
                v.wait_ge(*K.full(("modT",)))
                mt = B(("modT",), 4 * KD).rearrange("p (k s) -> p k s", s=2)
                nc.vector.tensor_copy(mcol[:, 0:KD, :], mt[:, 0:KD, :])
                nc.vector.scalar_tensor_tensor(mcol[:, KD:2 * KD, :], mt[:, KD:2 * KD, :], 1.0,
                                               gpre[:, :].unsqueeze(2).to_broadcast([P, KD, 2]), ALU.add, ALU.mult
                                               ).then_inc(*K.drained(("modT",)))
                for s in range(2):
                    for half in range(2):
                        job = ("gate_row", s, half)
                        v.wait_ge(*K.full(job))
                        tt(at(SGH + s * D + half * 512, 512), B(job), at(A_NPOST + half * 512, 512), ALU.mult
                           ).then_inc(*K.drained(job))
                stage_end(v)

                for t in range(TT + 2):
                    if t < TT:
                        v.wait_ge(*S.at("x_squares", t))
                        rstd(("x", t), (st[:, t:t + 1], D))
                        nc.vector.tensor_scalar(at(XN + (t % 4) * D, D), at(XN + (t % 4) * D, D), st[:, t:t + 1],
                                                None, ALU.mult).then_inc(*S.up("x_normed", t))
                    if t >= 2:
                        job, s = ("xT", t - 2, 1), int(t - 2 == NT)
                        v.wait_ge(*K.full(job))
                        for k in range(4):
                            last = nc.vector.tensor_scalar(hT[:, 4 + k, (t - 2) * P:(t - 1) * P], B(job)[:, k * P:(k + 1) * P],
                                                           mcol[:, KD + 4 + k, s:s + 1], mcol[:, 4 + k, s:s + 1],
                                                           ALU.mult, ALU.add)
                        last.then_inc(*K.drained(job))
                stage_end(v)

                xv = at(XV, TT, 768)

                def drain_uT(f):
                    for g in (1, 2):
                        job, n = ("uT", f, g), (4 if g == 1 else 1)
                        v.wait_ge(*K.full(job))
                        nc.vector.tensor_copy(xv[:, 4 * g:4 * g + n, f * P:(f + 1) * P],
                                              B(job, n * P).rearrange("p (a n) -> p a n", a=n)).then_inc(*K.drained(job))

                for f in range(6):
                    u, c = U0 + (f % 2) * UW, CU + (f % 2) * TOK
                    v.wait_ge(*S.at("middle_tap", f))
                    v.wait_ge(*S.at("edges", f))
                    for tap, shift in ((0, 0), (2, 2)):
                        ins = [nc.vector.scalar_tensor_tensor(at(c, D), at(u + shift * P, D), hcw[:, f, tap:tap + 1],
                                                              at(c, D), ALU.mult, ALU.add),
                               nc.vector.scalar_tensor_tensor(at(c + D, P), at(u + 10 * P + shift, P),
                                                              hcw[:, f, tap:tap + 1], at(c + D, P), ALU.mult, ALU.add)]
                        if tap == 0:
                            link(ins[1])
                        else:
                            ins[1].then_inc(*S.up("taps", f))
                    if f >= 1:
                        drain_uT(f - 1)

                def finish_gate(grp, t, dst, c0=0):
                    job = ("gate", grp, t)
                    v.wait_ge(*S.at("half_tanh", (grp, t)))
                    th = (GATE_T if grp in ("hy", "mla") else OB) + (t % 2) * GW
                    nc.vector.scalar_tensor_tensor(at(dst + t * GW, GW), at(th, GW), 1.0, B(job)[:, c0:c0 + GW],
                                                   ALU.add, ALU.mult).then_inc(*K.drained(job))

                v.wait_ge(*S.at("gate_rows_kept"))
                for t in range(2):
                    finish_gate("hy", t, SGH)
                drain_uT(5)
                stage_end(v)

                zv = at(XV, TT, 3, GW)
                for o in range(2):
                    if o == 1:
                        v.wait_ge(*K.full(("Y", 0, 3)))
                    for a0 in range(4):
                        job = ("Z", o, a0, 1)
                        v.wait_ge(*K.full(job))
                        nc.vector.tensor_copy(at(B2 + (a0 * 2 + 1) * 512, 512), B(job)).then_inc(*K.drained(job))
                    for a0 in range(4):
                        for p in range(2):
                            v.wait_ge(*K.emptied(("Z", o, a0, p)))
                    butterfly(("X", o), B2, B3, B2, -1)
                    if o == 1:
                        v.wait_ge(*S.at("spectrum1_back"))
                    def finish_gates(t0, t1):
                        for t in range(t0, t1):
                            if o == 1:
                                finish_gate("mla", t, SG)
                            elif t >= 2:
                                finish_gate("hy", t, SGH)

                    finish_gates(0, 3)
                    v.wait_ge(*S.at("butterfly_pool", ("X", o)))
                    H, X, T1 = (at(off, 8, 2, GW) for off in (HS, B2, B3))
                    h4 = slice(0, 4)
                    link(tt(T1[:, h4, :, :], H[:, h4, :, :], X[:, h4, :, :], ALU.mult))
                    link(tt(T1[:, h4, 0, :], T1[:, h4, 0, :], T1[:, h4, 1, :], ALU.subtract))
                    tt(T1[:, h4, 1, :], H[:, h4, 0, :], X[:, h4, 1, :], ALU.mult)
                    link(tt(X[:, h4, 0, :], H[:, h4, 1, :], X[:, h4, 0, :], ALU.mult))
                    link(tt(T1[:, h4, 1, :], T1[:, h4, 1, :], X[:, h4, 0, :], ALU.add), "product_rows_vector", o)
                    v.wait_ge(*K.emptied(("Zp", o)))
                    Hp, Xp, Tp = (at(off + 4096, 2, GW) for off in (HS, B2, B3))
                    link(tt(Tp[:, :, :], Hp[:, :, :], Xp[:, :, :], ALU.mult))
                    link(tt(Tp[:, 0, :], Tp[:, 0, :], Tp[:, 1, :], ALU.subtract))
                    tt(Tp[:, 1, :], Hp[:, 0, :], Xp[:, 1, :], ALU.mult)
                    link(tt(Xp[:, 0, :], Hp[:, 1, :], Xp[:, 0, :], ALU.mult), "product_vector", o)
                    tt(Tp[:, 1, :], Tp[:, 1, :], Xp[:, 0, :], ALU.add).then_inc(*S.up("product_prompt", o))
                    finish_gates(3, 6)
                    v.wait_ge(*S.at("product_pool", o))
                    butterfly(("G", o), B3, B2, B3, 1)
                    finish_gates(6, TT)
                    for i in range(4):
                        job = ("Y", o, i)
                        v.wait_ge(*K.full(job))
                        tt(zv[:, 2 * i:2 * i + 2, 2, :], B(job).rearrange("p (a n) -> p a n", a=2),
                           zv[:, 2 * i:2 * i + 2, o, :], ALU.mult).then_inc(*K.drained(job))
                    v.wait_ge(*K.full(("Yp", o)))
                    tt(zv[:, NT, 2, :], B(("Yp", o), GW), zv[:, NT, o, :], ALU.mult).then_inc(*K.drained(("Yp", o)))
                for t in range(TT):
                    v.wait_ge(*K.emptied(("Y", 1, t // 2) if t < NT else ("Yp", 1)))
                    nc.vector.scalar_tensor_tensor(zv[:, t, 2, :], zv[:, t, 2, :], 0.5, at(SGH + t * GW, GW),
                                                   ALU.mult, ALU.mult).then_inc(*S.up("gated", ("hy", t)))
                stage_end(v)

                def rope(x, heads, n, t, key):
                    m = n // 4
                    tab = ROPE + t * 192 + (0 if n == 32 else 64)
                    cos, sin = at(tab, n), at(tab + n, n)
                    t1 = at(ROT, heads, n)
                    t2 = at(ROT + 512, heads, n)
                    tt(t1, x, cos.unsqueeze(1).to_broadcast([P, heads, n]), ALU.mult)
                    for s in range(2):
                        for j in range(2):
                            a, b = (2 * s + j) * m, (2 * s + 1 - j) * m
                            last = tt(t2[:, :, a:a + m], x[:, :, b:b + m],
                                      sin[:, a:a + m].unsqueeze(1).to_broadcast([P, heads, m]), ALU.mult)
                    link(last)
                    link(tt(x, t1, t2, ALU.add), *key)

                def attention(grp):
                    two = NMAPS[grp] == 2
                    units, heads = UNITS[grp], HEADS[grp]
                    NU, NH = len(units), len(heads)
                    scale = DK[grp] ** -0.5

                    def maximum(i, s):
                        t, _ = units[i]
                        nk = n_keys(t) * P
                        col = 16 * (i % 4) + 8 * s
                        v.wait_ge(*K.full(("S", grp, i, s)))
                        link(nc.vector.tensor_reduce(st[:, col:col + 1], score_view(s if two else i % 2, nk),
                                                     AX.X, ALU.max))
                        nc.vector.tensor_scalar(st[:, col + 1:col + 2], st[:, col:col + 1], -scale, None, ALU.mult
                                                ).then_inc(*S.up("neg_max", (grp, i, s)))

                    def turned(i):
                        t, _ = units[i]
                        if i >= 2:
                            v.wait_ge(*K.full(("O", grp, i - 2)))
                        pt = PT + (i % 2) * TOK
                        job = ("T", grp, i)
                        v.wait_ge(*K.full(job))
                        if t == NT:
                            nc.vector.tensor_copy(at(pt, P), score_view(i % 2, P)).then_inc(*K.drained(job))
                        else:
                            nc.vector.tensor_copy(at(pt + 512, TOK - 512), score_view(i % 2, TOK)[:, 512:TOK]
                                                  ).then_inc(*K.drained(job))

                    def combine(i):
                        n = n_keys(units[i][0]) * P
                        c0, c1 = 16 * (i % 4), 16 * (i % 4) + 8
                        for s in range(2):
                            v.wait_ge(*K.emptied(("S", grp, i, s)))
                        link(nc.vector.reciprocal(st[:, c1 + 3:c1 + 4], st[:, c1 + 2:c1 + 3]))
                        link(nc.vector.scalar_tensor_tensor(st[:, c1 + 4:c1 + 5], st[:, c1 + 3:c1 + 4],
                                                            st[:, c0 + 2:c0 + 3], lamv[:, 6:7], ALU.mult, ALU.mult))
                        p0 = at(PB + (i % 2) * TOK, n)
                        nc.vector.scalar_tensor_tensor(p0, at(PB + 2 * TOK, n), st[:, c1 + 4:c1 + 5], p0,
                                                       ALU.mult, ALU.add).then_inc(*S.up("combined", (grp, i)))

                    def finish(i):
                        t, h = units[i]
                        c0 = 16 * (i % 4)
                        rc = st[:, c0 + 5:c0 + 6]
                        v.wait_ge(*K.emptied(("S", grp, i, 0)))
                        link(nc.vector.reciprocal(rc, st[:, c0 + 2:c0 + 3]))
                        v.wait_ge(*K.full(("O", grp, i)))
                        if h == heads[0] and t >= 2:
                            v.wait_ge(*K.full(("oT", grp, t - 2)))
                        o = OB + (t % 2) * GW
                        nc.vector.tensor_scalar(at(o + heads.index(h) * 64, 64), B(("O", grp, i), 64), rc, None, ALU.mult
                                                ).then_inc(*K.drained(("O", grp, i)))

                    def finish_tile(i):
                        t, h = units[i]
                        o = OB + (t % 2) * GW
                        if h != heads[-1]:
                            return
                        v.wait_ge(*K.emptied(("O", grp, i)))
                        if two:
                            r4 = st[:, 64:66]
                            sq = at(QS, P)
                            link(tt(sq, at(o, P), at(o, P), ALU.mult))
                            link(nc.vector.tensor_reduce(r4, at(QS, NH, 64), AX.X, ALU.add))
                            rstd((grp, t), (r4, 64))
                            link(tt(at(o, NH, 64), at(o, NH, 64), r4.unsqueeze(2).to_broadcast([P, NH, 64]), ALU.mult))
                            link(tt(at(o, NH, 64), at(o, NH, 64),
                                    at(WQB, 64).unsqueeze(1).to_broadcast([P, NH, 64]), ALU.mult))
                        sg = SG + t * GW + (64 * heads[0] if two else 0)
                        nc.vector.scalar_tensor_tensor(at(o, 64 * NH), at(o, 64 * NH), 0.5, at(sg, 64 * NH),
                                                       ALU.mult, ALU.mult).then_inc(*S.up("gated", (grp, t)))

                    for i in range(NU + 2):
                        if i < NU:
                            maximum(i, 0)
                        if two and 1 <= i <= NU:
                            combine(i - 1)
                        if two and i < NU:
                            maximum(i, 1)
                        if two and i >= 2:
                            finish(i - 2)
                        if two and i >= 2:
                            finish_tile(i - 2)
                        if not two and 1 <= i <= NU:
                            turned(i - 1)
                        if not two and 2 <= i:
                            finish(i - 2)
                            finish_tile(i - 2)

                v.wait_ge(*S.at("mla_params"))
                v.wait_ge(*S.at("mla_gains"))

                def latent_turned(t):
                    job = ("cT", t)
                    v.wait_ge(*K.full(job))
                    if t >= 1:
                        v.wait_ge(*K.full(("kv", t - 1)))
                    if t == TT:
                        nc.vector.tensor_copy(at(CT + 2 * P, P), B(job)[:, 2 * P:3 * P]).then_inc(*K.drained(job))
                        return
                    for i in range(3):
                        last = nc.vector.tensor_scalar(at(CT + i * P, P), B(job)[:, i * P:(i + 1) * P], mg[:, i:i + 1],
                                                       None, ALU.mult)
                    last.then_inc(*K.drained(job))

                for i in range(TT + 3):
                    if 1 <= i <= TT:
                        latent_turned(i - 1)
                    if i < TT:
                        c, z = 4 * (i % 2), ZB + (i % 2) * WC
                        v.wait_ge(*S.at("latent_squares", i))
                        rstd(("latent", i), (st[:, c:c + 1], 256), (st[:, c + 1:c + 2], P))
                        link(nc.vector.tensor_scalar(at(z, GW), at(z, GW), st[:, c:c + 1], None, ALU.mult))
                        link(nc.vector.tensor_scalar(at(z + GW, P), at(z + GW, P), st[:, c + 1:c + 2], None, ALU.mult),
                             "latent", i)
                        if i < NT:
                            rope(at(z + 384, 1, 32), 1, 32, i, ("k_roped", i))
                        else:
                            tt(at(CKVOUT, P), at(z + GW, P), at(KVGAIN, P), ALU.mult).then_inc(*S.up("state_ready", "mla"))
                    if i == TT:
                        nc.vector.memset(st[:, 73:74], 0.0).then_inc(*S.up("latent", TT))
                    if i == TT + 1:
                        latent_turned(TT)
                    if 2 <= i <= TT + 2:
                        t = i - 2
                        job = ("kT", t)
                        kt = CACHE if t == TT else key_tile(t)
                        v.wait_ge(*K.full(job))
                        nc.vector.tensor_copy(at(KT, MLA_HEADS, NKEY * P, parts=96)[:, :, kt * P:(kt + 1) * P],
                                              B(job, parts=96).rearrange("p (h n) -> p h n", h=MLA_HEADS)).then_inc(*K.drained(job))
                    if 1 <= i <= TT:
                        t = i - 1
                        v.wait_ge(*K.emptied(("q", t)))
                        if t < NT:
                            rope(at(QS, MLA_HEADS, 96)[:, :, 64:96], MLA_HEADS, 32, t, ("q_roped", t))
                        else:
                            nc.vector.memset(st[:, 72:73], 0.0).then_inc(*S.up("q_roped", t))
                attention("mla")
                stage_end(v)

                def split(grp, t, x, q, k):
                    sp_t = split_buf[:, (t % 2) * 896:(t % 2) * 896 + SPLIT_W[grp]]
                    if t >= 2:
                        v.wait_ge(*K.full(("kT", grp, t - 2)))
                    n = 64 if grp == "gqa" else 32
                    if grp == "gqa":
                        qd = sp_t[:, 0:512].rearrange("p (a b n) -> p a b n", a=4, b=2)
                        kd = sp_t[:, 512:896].rearrange("p (a b n) -> p a b n", a=2, b=3)
                        qh, ql = qd[:, :, 0, :], qd[:, :, 1, :]
                    else:
                        qd = sp_t[:, 0:384].rearrange("p (a b n) -> p a b n", a=4, b=3)
                        kd = sp_t[:, 384:768].rearrange("p (a b n) -> p a b n", a=4, b=3)
                        qh, ql = qd[:, :, 0, :], qd[:, :, 1, :]
                    nk = kd.shape[1]
                    if q is not None:
                        nc.vector.tensor_copy(qh, q)
                        if grp != "gqa":
                            nc.vector.tensor_copy(qd[:, :, 2, :], q)
                    nc.vector.tensor_copy(kd[:, :, 1, :], k)
                    link(nc.vector.tensor_copy(kd[:, :, 0, :], k))
                    if q is not None:
                        tt(ql, q, qh.bitcast(F32), ALU.subtract)
                    tt(kd[:, :, 2, :], k, kd[:, :, 0, :].bitcast(F32), ALU.subtract).then_inc(*S.up("split", (grp, t)))

                for grp, nh, n in (("gqa", 6, 64), ("diff0", 8, 32), ("diff1", 8, 32)):
                    if grp != "diff1":
                        v.wait_ge(*S.at(f"{grp[:4]}_params"))
                    if grp == "diff0":
                        q = at(WQB + 64, 4, 32)
                        for i in range(2):
                            link(tt(at(SQ + 32 * i, 32), q[:, 2 * i, :], q[:, 2 * i + 1, :], ALU.mult))
                        nc.vector.tensor_reduce(lamv[:, 0:2], at(SQ, 2, 32), AX.X, ALU.add).then_inc(*S.up("lambda_sums"))
                        link(nc.vector.tensor_scalar(at(WQB, 64), at(WQB, 64), lamv[:, 5:6], None, ALU.mult))
                    for i in range(TT + 1):
                        if i == TT:
                            if grp != "gqa":
                                v.wait_ge(*S.at(f"{grp}_cache"))
                            split(grp, TT, CKEY, None, at(CKEY, P // n, n))
                            continue
                        z = ZB + (i % 2) * WC
                        v.wait_ge(*K.emptied(("proj", grp, i)))
                        if grp == "gqa":
                            r6 = st[:, 8 * (i % 2):8 * (i % 2) + 6]
                            link(tt(at(SQ, 384), at(z, 384), at(z, 384), ALU.mult))
                            link(nc.vector.tensor_reduce(r6, at(SQ, 6, 64), AX.X, ALU.add))
                            rstd(("heads", i), (r6, 64))
                            link(tt(at(z, 6, 64), at(z, 6, 64), r6.unsqueeze(2).to_broadcast([P, 6, 64]), ALU.mult))
                            link(tt(at(z, 384), at(z, 384), at(WQB, 384), ALU.mult))
                        if i < NT:
                            rope(at(z, nh, n), nh, n, i, ("vector_step", None))
                        nq = 4
                        split(grp, i, z, at(z, nq, n), at(z + nq * n, nh - nq, n))
                        if i == NT:
                            nc.vector.memset(st[:, 72:73], 0.0).then_inc(*S.up("state_ready", grp))
                    if grp != "diff1":
                        for t in range(TT):
                            finish_gate(grp[:4], t, SG, 0 if grp == "gqa" else GW)
                    if grp == "diff0":
                        v.wait_ge(*S.at("lambda_exps"))
                        link(tt(lamv[:, 6:7], lamv[:, 3:4], lamv[:, 2:3], ALU.subtract))
                        link(tt(lamv[:, 6:7], lamv[:, 6:7], lamv[:, 4:5], ALU.subtract))
                    attention(grp)
                    stage_end(v)

                v.wait_ge(*S.at("gate_rows_back"))
                for t in range(TT):
                    c = 8 * (t % 2)
                    s = int(t == NT)
                    v.wait_ge(*S.at("out_squares", (t, 1)))
                    link(tt(st[:, c + 2:c + 3], st[:, c:c + 1], st[:, c + 1:c + 2], ALU.add))
                    rstd(("out", t), (st[:, c + 2:c + 3], D))
                    if t >= 2:
                        v.wait_ge(*S.at("x_updated", t - 2))
                    for half in range(2):
                        job = ("y", t, half)
                        nc.vector.scalar_tensor_tensor(at(YN + (t % 2) * D + half * 512, 512), B(job), st[:, c + 2:c + 3],
                                                       at(GR + s * D + half * 512, 512), ALU.mult, ALU.mult
                                                       ).then_inc(*K.drained(job))
                stage_end(v)
                layer_end(v)

        @block.gpsimd
        def _(pool):
            def link(ins, name="pool_step", key=None):
                ins.then_inc(*S.up(name, key))
                pool.wait_ge(*S.now(name))

            def tt(out, a, b, op):
                return nc.gpsimd.tensor_tensor(out, a, b, op)

            def inverse_root(key, x):
                pool.wait_ge(*S.at("variance", key))
                tt(x, x, mhalf[:, 0:x.shape[1]], ALU.pow).then_inc(*S.up("inverse_root", key))

            nc.gpsimd.memset(mhalf[:, :], -0.5).then_inc(S.raw("exponent_set"), 1)
            pool.wait_ge(S.raw("exponent_set"), 1)
            with pool.Fori(0, DEPTH) as l:
                def butterfly(key, src, mid, dst, sign):
                    E, M, X = at(src, 4, 2, 2, GW), at(mid, 4, 2, 2, GW), at(dst, 4, 2, 2, GW)
                    link(tt(at(mid + 2 * D, 2 * D), at(src, 2 * D), at(src + 2 * D, 2 * D), ALU.subtract),
                         "butterfly_diffs", key)
                    if src == dst:
                        pool.wait_ge(*S.at("butterfly_sums", key))
                    lo, hi = (1, 3) if sign < 0 else (3, 1)
                    tt(X[:, lo, :, 0, :], M[:, 2, :, 0, :], M[:, 3, :, 1, :], ALU.add)
                    tt(X[:, lo, :, 1, :], M[:, 2, :, 1, :], M[:, 3, :, 0, :], ALU.subtract)
                    tt(X[:, hi, :, 0, :], M[:, 2, :, 0, :], M[:, 3, :, 1, :], ALU.subtract)
                    link(tt(X[:, hi, :, 1, :], M[:, 2, :, 1, :], M[:, 3, :, 0, :], ALU.add), "butterfly_pool", key)

                eo = at(EO, TT, 3, GW)
                for o in (1, 0):
                    for t in range(TT):
                        pool.wait_ge(*K.emptied(("f3", o, t)))
                        if t in (0, NT):
                            pool.wait_ge(*S.at("lag0_cleared", (o, t)))
                        last = nc.gpsimd.tensor_scalar(eo[:, t, 2, :], eo[:, t, 1, :], -1.0, None, ALU.mult)
                    last.then_inc(*S.up("filter_negated", o))
                    for a0 in range(4):
                        for p in range(2):
                            pool.wait_ge(*K.emptied(("FE", o, a0, p)))
                    pool.wait_ge(*S.at("bias_added", (o, 1)))
                    if o == 0:
                        pool.wait_ge(*S.at("spectrum1_kept"))
                    butterfly(("F", o), B2, B3, HS, -1)
                stage_end(pool)
                for t in range(TT):
                    inverse_root(("x", t), st[:, t:t + 1])
                stage_end(pool)

                for half in range(2):
                    u = U0 + half * UW
                    nc.gpsimd.memset(at(u, 1), 0.0)
                    nc.gpsimd.memset(at(u + 9 * P + P - 1, 1), 0.0)
                    nc.gpsimd.memset(at(u + 10 * P, 1), 0.0)
                    link(nc.gpsimd.memset(at(u + 10 * P + 129, 1), 0.0))
                for f in range(6):
                    u = U0 + (f % 2) * UW
                    for i in range(3):
                        pool.wait_ge(*K.emptied(("u", f, i)))
                    nc.gpsimd.tensor_copy(at(u + 1, P - 1), at(u + 8 * P, P - 1))
                    nc.gpsimd.tensor_copy(at(u + 9 * P, P - 1), at(u + P + 1, P - 1)).then_inc(*S.up("edges", f))
                stage_end(pool)

                for o in range(2):
                    for a0 in range(4):
                        for p in range(2):
                            pool.wait_ge(*K.emptied(("Z", o, a0, p)))
                    butterfly(("X", o), B2, B3, B2, -1)
                    if o == 1:
                        pool.wait_ge(*S.at("spectrum1_back"))
                    pool.wait_ge(*S.at("butterfly_vector", ("X", o)))
                    H, X, T1 = (at(off, 8, 2, GW) for off in (HS, B2, B3))
                    h4 = slice(4, 8)
                    link(tt(T1[:, h4, :, :], H[:, h4, :, :], X[:, h4, :, :], ALU.mult))
                    link(tt(T1[:, h4, 0, :], T1[:, h4, 0, :], T1[:, h4, 1, :], ALU.subtract))
                    tt(T1[:, h4, 1, :], H[:, h4, 0, :], X[:, h4, 1, :], ALU.mult)
                    link(tt(X[:, h4, 0, :], H[:, h4, 1, :], X[:, h4, 0, :], ALU.mult))
                    link(tt(T1[:, h4, 1, :], T1[:, h4, 1, :], X[:, h4, 0, :], ALU.add), "product_pool", o)
                    pool.wait_ge(*S.at("product_rows_vector", o))
                    butterfly(("G", o), B3, B2, B3, 1)
                stage_end(pool)

                pool.wait_ge(*S.at("mla_params"))
                for t in range(TT + 1):
                    if t < TT:
                        inverse_root(("latent", t), st[:, 4 * (t % 2):4 * (t % 2) + 2])
                    if t < NT:
                        pool.wait_ge(*S.at("k_roped", t))
                    elif t == NT:
                        pool.wait_ge(*K.emptied(("proj", "mla", t)))
                    if t >= 1:
                        pool.wait_ge(*K.full(("kT", t - 1)))
                    src = at(CROPE, 32) if t == TT else at(ZB + (t % 2) * WC + 384, 32)
                    nc.gpsimd.tensor_copy(at(QS + 384, MLA_HEADS, 96)[:, :, 64:96],
                                          src.unsqueeze(1).to_broadcast([P, MLA_HEADS, 32])).then_inc(*S.up("k_rope_spread", t))
                stage_end(pool)
                for t in range(TT):
                    inverse_root(("heads", t), st[:, 8 * (t % 2):8 * (t % 2) + 6])
                stage_end(pool)

                for grp in ("diff0", "diff1"):
                    for t in range(TT):
                        inverse_root((grp, t), st[:, 64:66])
                    stage_end(pool)

                for t in range(TT):
                    inverse_root(("out", t), st[:, 8 * (t % 2) + 2:8 * (t % 2) + 3])
                    pool.wait_ge(*K.emptied(("y", t, 0)))
                    pool.wait_ge(*K.emptied(("y", t, 1)))
                    pool.wait_ge(*S.at(f"xr{t % 3}_loaded", t))
                    x = at(XR + (t % 3) * D, D)
                    tt(x, x, at(YN + (t % 2) * D, D), ALU.add).then_inc(*S.up("x_updated", t))
                stage_end(pool)
                layer_end(pool)

        return S.count, S.mark, K.jobs


def tables():
    f = np.float32
    token = (NT * np.arange(P)[:, None] + np.arange(NT)[None, :])
    row, col = (token // 64).astype(f), (token % 64).astype(f)

    def axial(n):
        m = n // 2
        inv = (f(10000.0) ** (-np.arange(0, m, 2, dtype=f) / f(m))).astype(f)
        cos, sin = [], []
        for pos in (row, col):
            ang = (pos[..., None] * inv).astype(f)
            cos += [np.cos(ang), np.cos(ang)]
            sin += [-np.sin(ang), np.sin(ang)]
        return np.concatenate(cos, -1), np.concatenate(sin, -1)

    c32, s32 = axial(32)
    c64, s64 = axial(64)
    rope = np.concatenate([c32, s32, c64, s64], -1).astype(f)

    def feats(n):
        t = np.linspace(0.0, 1.0, n, dtype=f)[:, None]
        w = (f(2.0 * math.pi) * np.arange(n, dtype=f)[:, None] / f(n)).astype(f)
        fr = np.linspace(1e-4, 15, 16, dtype=f)[None, :]
        return np.concatenate([t, np.cos(fr * w), -np.sin(fr * w)], -1).astype(f), t[:, 0]

    fs, ts = feats(N_SAMPLE)
    fp, tp = feats(N_PROMPT)
    order = token.T.reshape(-1)
    ft = np.concatenate([fs[order], fp], 0).T
    negt = -np.concatenate([ts[token], tp[:, None]], 1)
    f2 = np.arange(P)
    tab = np.zeros((P, NT, 2, 2, P))
    for a in range(NT):
        for p in range(2):
            ang = math.pi * (2 * (f2[None, :] + 256 * p) + 1) * (8 * np.arange(P)[:, None] + a) / 2048.0
            tab[:, a, p, 0, :], tab[:, a, p, 1, :] = np.cos(ang), -np.sin(ang)
    inv = tab.transpose(4, 1, 2, 3, 0)
    sel = np.zeros((2, 2, P), f)
    sel[0, 0], sel[1, 1] = 1, 1
    lam = np.array([[0.8 - 0.6 * math.exp(-0.3 * i), 1.0 - (0.8 - 0.6 * math.exp(-0.3 * i))] for i in range(DEPTH)], f)
    return {"rope": rope, "feats": ft.astype(f), "negt": negt.astype(f), "sel": sel,
            "tab_f": tab.reshape(P, -1).astype(f), "tab_i": inv.reshape(P, -1).astype(f),
            "ident": np.eye(P, dtype=f), "lam_init": lam}


DIRECT = ["cache_mla_ckv", "cache_mla_krope", "cache_gqa_k", "cache_gqa_v", "cache_diff_k", "cache_diff_v",
          "c", "c_ctx", "norm_pre", "norm_post", "ada_w", "ada_b", "w_in", "w_out", "mla_q_norm", "mla_wq_b",
          "mla_kv_norm", "mla_wkv_b", "gqa_q_norm", "gqa_k_norm", "diff_lq1", "diff_lk1", "diff_lq2", "diff_lk2",
          "diff_subln", "hy_conv_w", "hy_conv_b", "hy_fw1", "hy_fb1", "hy_fw2", "hy_fb2", "hy_fw3", "hy_freq",
          "hy_decay"]
OUTS = {"xs": (DEPTH + 1, TOK, D), "new_mla_ckv": (1, DEPTH, P, 128), "new_mla_krope": (1, DEPTH, P, 32),
        "new_gqa_k": (1, DEPTH, P, 2, 64), "new_gqa_v": (1, DEPTH, P, 2, 64),
        "new_diff_k": (1, DEPTH, P, 4, 64), "new_diff_v": (1, DEPTH, P, 4, 64)}


def build(nc, arrays, known):
    ins = {n: nc.dram_tensor(f"in_{n}", list(a.shape), F32, kind="ExternalInput").ap() for n, a in arrays.items()}
    outs = {n: nc.dram_tensor(f"out_{n}", list(s), F32, kind="ExternalOutput").ap() for n, s in OUTS.items()}
    outs["spectrum_kept"] = nc.dram_tensor("spectrum_kept", [P, 4608], F32, kind="Internal").ap()
    outs["gates_kept"] = nc.dram_tensor("gates_kept", [P, 2 * D], F32, kind="Internal").ap()
    return program(nc, ins, outs, known)


def kernel(**inputs):
    import concourse.bacc as bacc
    from concourse.bass_utils import run_bass_kernel_spmd

    arrays = {n: np.ascontiguousarray(inputs[n]) for n in DIRECT}
    arrays["x"] = np.concatenate([np.asarray(inputs["x_sample"])[0], np.asarray(inputs["x_prompt"])[0]], 0)
    arrays["hy_bias2"] = np.ascontiguousarray(inputs["hy_bias"]).reshape(DEPTH, 512)
    arrays.update(tables())
    known = None
    for _ in range(2):
        nc = bacc.Bacc("TRN2", target_bir_lowering=False, num_devices=1)
        known = build(nc, arrays, known)
    r = run_bass_kernel_spmd(nc, [{f"in_{n}": a for n, a in arrays.items()}], core_ids=[0]).results[0]
    x = r["out_xs"][DEPTH]
    return (x[NT * P:][None], x[:NT * P][None]) + tuple(r[f"out_{n}"] for n in list(OUTS)[1:])
```
